# Optimizing a Trainium2 kernel written in Bass

```python
import jax, jax.numpy as jnp
from jax import lax
import numpy as np

D_MODEL = 1024
BATCH = 1
SEQ = 2048
DEPTH = 1

GRID_W = 64
FNET_GROUPS = 4
FNET_GROUP_DIM = 128
FNET_WIDTH = FNET_GROUPS * FNET_GROUP_DIM
NA_HEADS = 8
NA_HEAD_DIM = 64
NA_WIDTH = NA_HEADS * NA_HEAD_DIM
NA_ROW_WIN = 8
NA_COL_WIN = 16
RPB_ROWS = 2 * NA_ROW_WIN - 1
RPB_COLS = 2 * NA_COL_WIN - 1
N_BRANCHES = 2
IN_WIDTH = FNET_WIDTH + 3 * NA_WIDTH + N_BRANCHES * D_MODEL
D_FF = 2816
CONV_W = 3
RMS_EPS = 1e-6

kernel_name = "fnet_natten_gated_hybrid_encoder"

def rms_norm(x, g):
    xf = x.astype(jnp.float32)
    y = xf * lax.rsqrt(jnp.mean(xf * xf, axis=-1, keepdims=True) + RMS_EPS)
    return (y * g.astype(jnp.float32)).astype(x.dtype)

def fourier_mix(u):
    b, s, _ = u.shape
    ug = u.reshape(b, s, FNET_GROUPS, FNET_GROUP_DIM).astype(jnp.float32)
    f = jnp.fft.fft2(ug, axes=(1, 3), norm="ortho").real
    return f.reshape(b, s, FNET_WIDTH).astype(u.dtype)

def neighbourhood_attention(q, k, v, rpb):
    b, s, _ = q.shape
    rows = s // GRID_W
    kr = min(NA_ROW_WIN, rows)
    shp = (b, rows, GRID_W, NA_HEADS, NA_HEAD_DIM)
    q = q.reshape(shp) * (NA_HEAD_DIM ** -0.5)
    k = k.reshape(shp)
    v = v.reshape(shp)
    cols = jnp.arange(GRID_W)
    col_start = jnp.clip(cols - NA_COL_WIN // 2, 0, GRID_W - NA_COL_WIN)
    col_idx = col_start[:, None] + jnp.arange(NA_COL_WIN)[None, :]
    dc = col_idx - cols[:, None] + (NA_COL_WIN - 1)
    rpb32 = rpb.astype(jnp.float32)

    def row_block(r):
        rs = jnp.clip(r - kr // 2, 0, rows - kr)
        q_r = lax.dynamic_index_in_dim(q, r, axis=1, keepdims=False)
        k_r = lax.dynamic_slice_in_dim(k, rs, kr, axis=1)[:, :, col_idx]
        v_r = lax.dynamic_slice_in_dim(v, rs, kr, axis=1)[:, :, col_idx]
        dr = rs + jnp.arange(kr) - r + (NA_ROW_WIN - 1)
        bias = rpb32[:, dr[None, :, None], dc[:, None, :]]
        sc = jnp.einsum('bqhd,brqwhd->bhqrw', q_r, k_r).astype(jnp.float32) + bias[None]
        p = jax.nn.softmax(sc.reshape(b, NA_HEADS, GRID_W, kr * NA_COL_WIN), axis=-1)
        p = p.reshape(b, NA_HEADS, GRID_W, kr, NA_COL_WIN).astype(v.dtype)
        return jnp.einsum('bhqrw,brqwhd->bqhd', p, v_r)

    out = lax.map(row_block, jnp.arange(rows))
    return jnp.transpose(out, (1, 0, 2, 3, 4)).reshape(b, s, NA_WIDTH)

def depthwise_conv_seq(u, w, bias):
    s = u.shape[1]
    pad = CONV_W // 2
    up = jnp.pad(u, ((0, 0), (pad, CONV_W - 1 - pad), (0, 0)))
    out = bias
    for j in range(CONV_W):
        out = out + up[:, j:j + s] * w[j]
    return out

def hybrid_layer(x, norm1_g, w_in, b_gate, rpb, w_fa, w_nb, w_out,
                 norm2_g, w_up, conv_w, conv_b, w_down):
    b, s, _ = x.shape
    h = rms_norm(x, norm1_g)
    proj = h @ w_in
    o1 = FNET_WIDTH
    o2 = o1 + NA_WIDTH
    o3 = o2 + NA_WIDTH
    o4 = o3 + NA_WIDTH
    u_f, q, k, v, g = jnp.split(proj, [o1, o2, o3, o4], axis=-1)
    g = jax.nn.sigmoid(g.reshape(b, s, N_BRANCHES, D_MODEL) + b_gate)
    a_branch = fourier_mix(u_f) @ w_fa
    n_branch = neighbourhood_attention(q, k, v, rpb) @ w_nb
    mixed = g[:, :, 0] * a_branch + g[:, :, 1] * n_branch
    x = x + mixed @ w_out
    h2 = rms_norm(x, norm2_g)
    up = depthwise_conv_seq(h2 @ w_up, conv_w, conv_b)
    val, gate = jnp.split(up, 2, axis=-1)
    x = x + (jax.nn.silu(gate) * val) @ w_down
    return x

def setup_inputs(seed: int = 0) -> dict:
    key = jax.random.key(seed)
    ks = jax.random.split(key, 16)
    f32 = jnp.float32
    L, D = DEPTH, D_MODEL
    nrm = lambda k, shape, scale: jax.random.normal(k, shape, f32) * scale
    return {
        "x": jax.random.normal(ks[0], (BATCH, SEQ, D), f32),
        "norm1_g": 1.0 + nrm(ks[1], (L, D), 0.05),
        "w_in": nrm(ks[2], (L, D, IN_WIDTH), D ** -0.5),
        "b_gate": nrm(ks[3], (L, N_BRANCHES, D), 0.1),
        "rpb": nrm(ks[4], (L, NA_HEADS, RPB_ROWS, RPB_COLS), 0.5),
        "w_fa": nrm(ks[5], (L, FNET_WIDTH, D), FNET_WIDTH ** -0.5),
        "w_nb": nrm(ks[6], (L, NA_WIDTH, D), NA_WIDTH ** -0.5),
        "w_out": nrm(ks[7], (L, D, D), D ** -0.5),
        "norm2_g": 1.0 + nrm(ks[8], (L, D), 0.05),
        "w_up": nrm(ks[9], (L, D, 2 * D_FF), D ** -0.5),
        "conv_w": nrm(ks[10], (L, CONV_W, 2 * D_FF), CONV_W ** -0.5),
        "conv_b": nrm(ks[11], (L, 2 * D_FF), 0.02),
        "w_down": nrm(ks[12], (L, D_FF, D), D_FF ** -0.5),
        "final_g": 1.0 + nrm(ks[13], (D,), 0.05),
    }

def reference(x, norm1_g, w_in, b_gate, rpb, w_fa, w_nb, w_out,
              norm2_g, w_up, conv_w, conv_b, w_down, final_g):
    for l in range(DEPTH):
        x = hybrid_layer(x, norm1_g[l], w_in[l], b_gate[l], rpb[l], w_fa[l], w_nb[l], w_out[l],
                         norm2_g[l], w_up[l], conv_w[l], conv_b[l], w_down[l])
    return rms_norm(x, final_g)


_drawn_inputs = setup_inputs


def setup_inputs(seed=0):
    import zlib

    import numpy as np

    out = dict(_drawn_inputs(seed))
    spreads = {}
    factors = {'b_gate': 3.641, 'conv_b': 4.155}
    for name, (base, spread) in spreads.items():
        noise = np.random.default_rng([zlib.crc32(name.encode()), seed]).standard_normal(out[name].shape)
        drawn = base * np.exp(spread * noise) if base else spread * noise
        out[name] = __import__('jax').numpy.asarray(drawn.astype(out[name].dtype))
    for name, factor in factors.items():
        out[name] = (out[name] * factor).astype(out[name].dtype)
    return out
```

```python
from contextlib import ExitStack

import numpy as np

import concourse.bass as bass
from concourse import mybir

F32 = mybir.dt.float32
F32R = mybir.dt.float32r
BF16 = mybir.dt.bfloat16
ALU = mybir.AluOpType
ACT = mybir.ActivationFunctionType
AX = mybir.AxisListType

P = 128
D = 1024
SEQ = 2048
KD = D // P
NTOK = SEQ // P
BLK = 512
NBLK = SEQ // BLK
TPB = BLK // P
GRID_W = 64
FNET_GROUPS, FNET_DIM = 4, 128
FNET_W = FNET_GROUPS * FNET_DIM
HEADS, HEAD_DIM = 8, 64
NA_W = HEADS * HEAD_DIM
ROW_WIN, COL_WIN = 8, 16
D_FF = 2816
EPS = 1e-6
BANKS = 8
QR, QC = 8, 16


def f32(ap):
    return ap.bitcast(F32)


SPLIT = ((0, 0), (0, 1), (1, 0))


class Pool:

    def __init__(self, nc, ctx, tag):
        self.nc, self.ctx, self.tag = nc, ctx, tag

    def sb(self, name, shape, dt=F32):
        return self.ctx.enter_context(self.nc.sbuf_tensor(f"{self.tag}_{name}", shape, dt))

    def banks(self):
        return self.ctx.enter_context(self.nc.psum_tensor(f"{self.tag}_psum", [P, BANKS, BLK], F32))

    def sem(self, name):
        return self.ctx.enter_context(self.nc.semaphore(f"{self.tag}_{name}"))

    def sems(self, name, n):
        return [self.sem(f"{name}{i}") for i in range(n)]


def input_phase(nc, x, w_in, norm_g, b_gate, eye, u_out, qT_out, v_out, kT_out, gT_out):
    RAW, STAGES, XS = 2, 4, 3
    with ExitStack() as ctx:
        m = Pool(nc, ctx, "in")
        hT = m.sb("hT", [P, 2, KD, SEQ], F32R)
        w = m.sb("w", [P, 2, 6, KD, P], F32R)
        wraw = m.sb("wraw", [P, RAW, KD, P])
        stage = m.sb("stage", [P, STAGES, BLK])
        xt = m.sb("xt", [P, XS, D])
        square = m.sb("square", [P, D], BF16)
        ident = m.sb("ident", [P, P])
        gain = m.sb("gain", [P, KD])
        gbias = m.sb("gbias", [P, 2 * KD])
        bias_now = m.sb("bias_now", [P, 2])
        sumsq = m.sb("sumsq", [P, NTOK])
        mean = m.sb("mean", [P, NTOK])
        root = m.sb("root", [P, NTOK])
        rstd = m.sb("rstd", [P, NTOK])
        corr = m.sb("corr", [P, NTOK])
        scale = m.sb("scale", [P, NTOK])
        ps = m.banks()

        const_in = m.sem("const_in")
        x_in = m.sems("x_in", XS)
        sumsq_done = m.sem("sumsq_done")
        mean_done = m.sem("mean_done")
        root_done = m.sem("root_done")
        x_scaled = m.sem("x_scaled")
        dve_step = m.sem("dve_step")
        x_turned = m.sem("x_turned")
        head_done = m.sem("head_done")
        tail_done = m.sem("tail_done")
        w_in_raw = m.sems("w_in_raw", RAW)
        w_head = m.sem("w_head")
        w_tail = m.sem("w_tail")
        mm_done = m.sem("mm_done")
        bias_ready = m.sem("bias_ready")
        evac_done = m.sem("evac_done")
        stored = m.sems("stored", STAGES)

        UQVK = 16
        NG = 16
        src_tile = [0, 1, 2, 3, 4, 5, 6, 7, 12, 13, 14, 15, 8, 9, 10, 11]
        slot = [0, 1, 2, 3, 4, 5, 4, 5, 0, 1, 2, 3, 4, 5, 4, 5]
        free_at = [0, 0, 0, 0, 0, 0, 20, 24, 16, 16, 16, 16, 28, 32, 52, 56]
        ng_evac = 16 + 16 + 16 + 16

        block = ctx.enter_context(nc.Block())

        @block.sync
        def _(sp):
            for dst, src in ((ident, eye), (gain, norm_g), (gbias, b_gate)):
                sp.dma_start(dst[:, :], src).then_inc(const_in, 16)

            def load_w(t):
                if t >= RAW:
                    sp.wait_ge(w_tail, t - RAW + 1)
                sp.dma_start(wraw[:, t % RAW], w_in[src_tile[t]]).then_inc(w_in_raw[t % RAW], 16)

            def store(n, dst):
                sp.wait_ge(evac_done, n + 1)
                sp.dma_start(dst, stage[:, n % STAGES]).then_inc(stored[n % STAGES], 16)

            for t in range(NTOK):
                if t >= XS:
                    sp.wait_ge(x_turned, t - XS + 1)
                sp.dma_start(xt[:, t % XS], x[t * P:(t + 1) * P, :]).then_inc(x_in[t % XS], 16)
                if t < 6:
                    load_w(t)
                if t > TPB:
                    n = t - TPB - 1
                    store(n, u_out[n * P:(n + 1) * P, :])
            for n in range(NTOK - TPB - 1, NTOK):
                store(n, u_out[n * P:(n + 1) * P, :])
            for t in range(6, 8):
                load_w(t)
            n = NTOK
            for q in range(4):
                load_w(8 + q)
                for b in range(NBLK):
                    store(n, qT_out[q * P:(q + 1) * P, b * BLK:(b + 1) * BLK])
                    n += 1
            for i in range(NTOK):
                if i % 4 == 0:
                    load_w(12 + i // 4)
                store(n, v_out[i * P:(i + 1) * P, :])
                n += 1

            def load_gate(t):
                sp.dma_start(wraw[:, t % RAW], w_in[16 + t]).then_inc(w_in_raw[t % RAW], 16)

            for q in range(4):
                if q >= 2:
                    sp.wait_ge(w_tail, UQVK + q - 2 - 1)
                    load_gate(q - 2)
                for b in range(NBLK):
                    store(n, kT_out[q * P:(q + 1) * P, b * BLK:(b + 1) * BLK])
                    n += 1
            with sp.Fori(0, NG // 2 - 1) as i:
                for j in range(2):
                    sp.wait_ge(w_tail, i * 2 + (UQVK + j + 1))
                    sp.dma_start(wraw[:, j], w_in[bass.ds(i * 2 + (18 + j), 1)].rearrange("o p k c -> (o p) k c")
                                 ).then_inc(w_in_raw[j], 16)
                    for b in range(NBLK):
                        sp.wait_ge(evac_done, i * 8 + (ng_evac + 4 * j + b + 1))
                        sp.dma_start(gT_out[bass.ds((i * 2 + j) * P, P), b * BLK:(b + 1) * BLK],
                                     stage[:, b]).then_inc(stored[b], 16)
            n = ng_evac + 4 * (NG - 2)
            for t in range(NG - 2, NG):
                for b in range(NBLK):
                    store(n, gT_out[t * P:(t + 1) * P, b * BLK:(b + 1) * BLK])
                    n += 1
            for s in range(STAGES):
                sp.wait_ge(stored[s], 16 * (n // STAGES))

        @block.gpsimd
        def _(pool):
            def tail(t, s):
                nc.gpsimd.tensor_tensor(w[:, 1, s], wraw[:, t % RAW], f32(w[:, 0, s]),
                                        ALU.subtract).then_inc(w_tail, 1)

            for t in range(UQVK):
                pool.wait_ge(w_head, t + 1)
                tail(t, slot[t])
            with pool.Fori(0, NG // 2) as i:
                for j in range(2):
                    pool.wait_ge(w_head, i * 2 + (UQVK + j + 1))
                    tail(j, 4 + j)

        @block.vector
        def _(dve):
            steps = [0]

            def after(ins):
                steps[0] += 1
                ins.then_inc(dve_step, 1)
                dve.wait_ge(dve_step, steps[0])

            def head(t):
                dve.wait_ge(w_in_raw[t % RAW], 16 * (t // RAW + 1))
                if free_at[t]:
                    dve.wait_ge(mm_done, free_at[t])
                nc.vector.tensor_copy(w[:, 0, slot[t]], wraw[:, t % RAW]).then_inc(w_head, 1)

            dve.wait_ge(const_in, 48)
            for t in range(NTOK):
                c = slice(t, t + 1)
                dve.wait_ge(sumsq_done, t + 1)
                nc.vector.tensor_scalar(mean[:, c], sumsq[:, c], 1.0 / D, EPS, ALU.mult, ALU.add).then_inc(mean_done, 1)
                dve.wait_ge(root_done, t + 1)
                after(nc.vector.reciprocal(rstd[:, c], root[:, c]))
                after(nc.vector.tensor_scalar(corr[:, c], rstd[:, c], rstd[:, c], mean[:, c], ALU.mult, ALU.mult))
                after(nc.vector.tensor_scalar(scale[:, c], corr[:, c], -0.5, 1.5, ALU.mult, ALU.add))
                after(nc.vector.tensor_tensor(rstd[:, c], rstd[:, c], scale[:, c], ALU.mult))
                nc.vector.tensor_scalar(xt[:, t % XS], xt[:, t % XS], rstd[:, c], None, ALU.mult).then_inc(x_scaled, 1)
                if t < 6:
                    head(t)
                if t % TPB == TPB - 1:
                    b = t // TPB
                    for k in range(KD):
                        dve.wait_ge(head_done, b * KD + k + 1)
                        dst = slice(b * BLK, (b + 1) * BLK)
                        nc.vector.scalar_tensor_tensor(
                            out=hT[:, 1, k, dst], in0=ps[:, k], scalar=gain[:, k:k + 1],
                            in1=f32(hT[:, 0, k, dst]), op0=ALU.mult, op1=ALU.subtract).then_inc(tail_done, 1)
            for t in range(6, UQVK):
                head(t)
            with dve.Fori(0, NG // 2) as i:
                for j in range(2):
                    dve.wait_ge(evac_done, i * 8 + (60 + 4 * j))
                    nc.vector.tensor_copy(bias_now[:, j:j + 1], gbias[:, bass.ds(i * 2 + j, 1)]).then_inc(bias_ready, 1)
                    dve.wait_ge(w_in_raw[j], i * 16 + 16 * (UQVK // 2 + 1))
                    dve.wait_ge(mm_done, i * 8 + (60 + 4 * j))
                    nc.vector.tensor_copy(w[:, 0, 4 + j], wraw[:, j]).then_inc(w_head, 1)

        @block.scalar
        def _(act):
            act.wait_ge(const_in, 48)
            n = 0

            def evac(n, func, **kw):
                act.wait_ge(mm_done, n + 1)
                if n >= STAGES:
                    act.wait_ge(stored[n % STAGES], 16 * (n // STAGES))
                nc.scalar.activation(stage[:, n % STAGES], ps[:, n % BANKS], func, **kw).then_inc(evac_done, 1)

            def stats(t):
                act.wait_ge(x_in[t % XS], 16 * (t // XS + 1))
                if t:
                    act.wait_ge(sumsq_done, t)
                nc.scalar.activation(square[:, :], xt[:, t % XS], ACT.Square,
                                     accum_out=sumsq[:, t:t + 1]).then_inc(sumsq_done, 1)
                act.wait_ge(mean_done, t + 1)
                nc.scalar.activation(root[:, t:t + 1], mean[:, t:t + 1], ACT.Sqrt).then_inc(root_done, 1)

            for t in range(TPB):
                stats(t)
            for b in range(NBLK):
                act.wait_ge(x_turned, (b + 1) * TPB)
                for k in range(KD):
                    nc.scalar.activation(hT[:, 0, k, b * BLK:(b + 1) * BLK], ps[:, k], ACT.Copy,
                                         scale=gain[:, k:k + 1]).then_inc(head_done, 1)
                for j in range(TPB):
                    evac(n, ACT.Copy)
                    n += 1
                    if b < NBLK - 1:
                        stats((b + 1) * TPB + j)
            for _ in range(16):
                act.wait_ge(mm_done, n + 1)
                act.wait_ge(stored[n % STAGES], 16 * (n // STAGES))
                nc.scalar.activation(stage[:, n % STAGES].rearrange("p (j b c) -> p j b c", b=QR, c=QC),
                                     ps[:, n % BANKS].rearrange("p (b j c) -> p j b c", b=QR, c=QC)[:, :, ::-1],
                                     ACT.Copy, scale=HEAD_DIM ** -0.5).then_inc(evac_done, 1)
                n += 1
            for _ in range(32):
                evac(n, ACT.Copy)
                n += 1
            with act.Fori(0, NG // 2) as i:
                for j in range(2):
                    act.wait_ge(bias_ready, i * 2 + (j + 1))
                    for b in range(NBLK):
                        act.wait_ge(mm_done, i * 8 + (ng_evac + 4 * j + b + 1))
                        act.wait_ge(stored[b], i * 32 + 16 * (ng_evac // 4 + j))
                        nc.scalar.activation(stage[:, b], ps[:, 4 * j + b], ACT.Sigmoid,
                                             bias=bias_now[:, j:j + 1]).then_inc(evac_done, 1)

        @block.tensor
        def _(pe):
            pe.wait_ge(const_in, 48)
            n = 0

            def slab(n, t):
                if n >= BANKS:
                    pe.wait_ge(evac_done, n - BANKS + 1)
                for k in range(KD):
                    for a, b in SPLIT:
                        last = nc.tensor.matmul(ps[:, n % BANKS], hT[:, a, k, t * P:(t + 1) * P], w[:, b, 0:4, k],
                                                start=(k == 0 and (a, b) == SPLIT[0]),
                                                stop=(k == KD - 1 and (a, b) == SPLIT[-1]))
                return last.then_inc(mm_done, 1)

            def tile(bank, s, b, first_wait):
                pe.wait_ge(evac_done, first_wait)
                for k in range(KD):
                    for a, c in SPLIT:
                        last = nc.tensor.matmul(ps[:, bank], w[:, a, s, k], hT[:, c, k, b * BLK:(b + 1) * BLK],
                                                start=(k == 0 and (a, c) == SPLIT[0]),
                                                stop=(k == KD - 1 and (a, c) == SPLIT[-1]))
                return last.then_inc(mm_done, 1)

            for b in range(NBLK):
                if b:
                    pe.wait_ge(evac_done, b * TPB)
                for t in range(b * TPB, (b + 1) * TPB):
                    pe.wait_ge(x_scaled, t + 1)
                    for k in range(KD):
                        last = nc.tensor.transpose(ps[:, k, (t % TPB) * P:(t % TPB + 1) * P],
                                                   xt[:, t % XS, k * P:(k + 1) * P], ident[:, :])
                    last.then_inc(x_turned, 1)
                pe.wait_ge(tail_done, (b + 1) * KD)
                if b == 0:
                    pe.wait_ge(w_tail, 4)
                for t in range(b * TPB, (b + 1) * TPB):
                    slab(n, t)
                    n += 1

            def narrow(t, s, n):
                pe.wait_ge(w_tail, t + 1)
                for b in range(NBLK):
                    tile((n + b) % BANKS, s, b, n + b - BANKS + 1)

            for q in range(4):
                narrow(4 + q, slot[4 + q], n + 4 * q)
            n += 16
            pe.wait_ge(w_tail, 12)
            for t in range(NTOK):
                slab(n + t, t)
            n += NTOK
            for q in range(4):
                narrow(12 + q, slot[12 + q], n + 4 * q)
            with pe.Fori(0, NG // 2) as i:
                for j in range(2):
                    pe.wait_ge(w_tail, i * 2 + (UQVK + j + 1))
                    for b in range(NBLK):
                        tile(4 * j + b, 4 + j, b, i * 8 + (ng_evac + 4 * j + b - BANKS + 1))


def fourier_phase(nc, u, pos_table, chan_table, fnT_out):
    A = SEQ // P
    CW = 256
    CHUNKS = FNET_W // CW
    GPC = CW // P
    ND = A // 2 + 1
    XB = (ND + 1) // 2
    ORTHO = 1.0 / float(np.sqrt(SEQ * FNET_DIM))
    c1, c2, c3 = (float(np.cos(np.pi * i / 8)) for i in (1, 2, 3))
    USES = XB + 6
    with ExitStack() as ctx:
        m = Pool(nc, ctx, "ft")
        ub = m.sb("u", [P, CHUNKS, A, CW])
        st = m.sb("st", [P, A, CW])
        s4 = m.sb("s4", [P, 8, CW])
        s2 = m.sb("s2", [P, 4, CW])
        ab = m.sb("ab", [P, 2, CW])
        mn = m.sb("mn", [P, 6, CW])
        tmp = m.sb("tmp", [P, 8, CW])
        Y = m.sb("Y", [P, 2, A, CW], F32R)
        traw = m.sb("traw", [P, A, 2 * P])
        tab = m.sb("tab", [P, 2, A, 2 * P], F32R)
        craw = m.sb("craw", [P, 2, P])
        ctab = m.sb("ctab", [P, 2, 2, P], F32R)
        X = m.sb("X", [P, 2, 2 * XB, 2, P], F32R)
        real = m.sb("real", [P, 2, BLK])
        out = m.sb("out", [P, 1, SEQ])
        ps = m.banks()

        tab_in, u_in = m.sem("tab_in"), m.sems("u_in", CHUNKS)
        tab_head, tab_tail = m.sem("tab_head"), m.sem("tab_tail")
        step = m.sem("step")
        y_ready, y_head, y_tail = m.sem("y_ready"), m.sem("y_head"), m.sem("y_tail")
        x_mm, x_head, x_tail = m.sem("x_mm"), m.sem("x_head"), m.sem("x_tail")
        out_mm, real_done, mirror_done = m.sem("out_mm"), m.sem("real_done"), m.sem("mirror_done")
        freed = m.sem("freed")
        stored = m.sem("stored")
        DS = [(0, 4), (4, 4), (8, 1)]

        block = ctx.enter_context(nc.Block())

        @block.sync
        def _(sp):
            u_v = u.rearrange("(a b) c -> b a c", b=P)
            sp.dma_start(ub[:, 0], u_v[:, :, 0:CW]).then_inc(u_in[0], 16)
            sp.dma_start(craw[:, :], chan_table).then_inc(tab_in, 16)
            sp.dma_start(traw[:, :], pos_table).then_inc(tab_in, 16)
            sp.dma_start(ub[:, 1], u_v[:, :, CW:2 * CW]).then_inc(u_in[1], 16)
            for g in range(FNET_GROUPS):
                sp.wait_ge(mirror_done, 3 * (g + 1))
                sp.dma_start(fnT_out[g * P:(g + 1) * P, :], out[:, 0]).then_inc(stored, 16)
            sp.wait_ge(stored, 16 * FNET_GROUPS)

        @block.gpsimd
        def _(pool):
            pool.wait_ge(tab_head, 1)
            nc.gpsimd.tensor_tensor(ctab[:, 1], craw[:, :], f32(ctab[:, 0]), ALU.subtract).then_inc(tab_tail, 1)
            pool.wait_ge(tab_head, 2)
            nc.gpsimd.tensor_tensor(tab[:, 1], traw[:, :], f32(tab[:, 0]), ALU.subtract).then_inc(tab_tail, 1)
            for h in range(CHUNKS):
                for e in range(2):
                    pool.wait_ge(y_head, 2 * h + e + 1)
                    nc.gpsimd.tensor_tensor(Y[:, 1, e::2], ub[:, h, e::2], f32(Y[:, 0, e::2]),
                                            ALU.subtract).then_inc(y_tail, 1)

        @block.vector
        def _(dve):
            V = nc.vector
            done = [0]

            def op(ins):
                done[0] += 1
                ins.then_inc(step, 1)
                return done[0]

            def after(n):
                dve.wait_ge(step, n)

            def mac(o, a, k, b, op1=ALU.add):
                return op(V.scalar_tensor_tensor(out=o, in0=a, scalar=k, in1=b, op0=ALU.mult, op1=op1))

            def tt(o, a, b, f):
                return op(V.tensor_tensor(o, a, b, f))

            def dft16(h):
                y = ub[:, h]
                dve.wait_ge(u_in[h], 16)
                if done[0]:
                    after(done[0])
                tt(st[:, 0:8], y[:, 0:8], y[:, 8:16], ALU.add)
                n = tt(st[:, 8:16], y[:, 0:8], y[:, 8:16], ALU.subtract)
                t = st[:, 8:16]
                after(n)
                tt(s4[:, 0:4], st[:, 0:4], st[:, 4:8], ALU.add)
                tt(s4[:, 4:8], st[:, 0:4], st[:, 4:8], ALU.subtract)
                tt(mn[:, 0:3], t[:, 1:4], t[:, 7:4:-1], ALU.subtract)
                n = tt(mn[:, 3:6], t[:, 1:4], t[:, 7:4:-1], ALU.add)
                after(n)
                tt(s2[:, 0:2], s4[:, 0:2], s4[:, 2:4], ALU.add)
                tt(y[:, 4:13:8], s4[:, 0:2], s4[:, 2:4], ALU.subtract)
                tt(ab[:, 0], s4[:, 5], s4[:, 7], ALU.subtract)
                n = tt(ab[:, 1], s4[:, 5], s4[:, 7], ALU.add)
                after(n)
                tt(y[:, 0], s2[:, 0], s2[:, 1], ALU.add)
                tt(y[:, 8], s2[:, 0], s2[:, 1], ALU.subtract)
                mac(y[:, 2], ab[:, 0], c2, s4[:, 4])
                mac(y[:, 6], ab[:, 0], -c2, s4[:, 4])
                mac(y[:, 10], ab[:, 1], c2, s4[:, 6])
                n = mac(y[:, 14], ab[:, 1], -c2, s4[:, 6])
                after(n)
                V.engine_nop().then_inc(y_ready, 1)
                mac(tmp[:, 0], mn[:, 1], c2, t[:, 0])
                mac(tmp[:, 1], mn[:, 1], -c2, t[:, 0])
                mac(tmp[:, 2], mn[:, 2], c3 / c1, mn[:, 0])
                mac(tmp[:, 3], mn[:, 2], -c1 / c3, mn[:, 0])
                mac(tmp[:, 4], mn[:, 4], c2, t[:, 4])
                mac(tmp[:, 5], mn[:, 4], c2, t[:, 4], ALU.subtract)
                mac(tmp[:, 6], mn[:, 5], -c3 / c1, mn[:, 3])
                n = mac(tmp[:, 7], mn[:, 3], c3 / c1, mn[:, 5])
                after(n)
                mac(y[:, 1], tmp[:, 2], c1, tmp[:, 0])
                mac(y[:, 7], tmp[:, 2], -c1, tmp[:, 0])
                mac(y[:, 3], tmp[:, 3], c3, tmp[:, 1])
                mac(y[:, 5], tmp[:, 3], -c3, tmp[:, 1])
                mac(y[:, 9], tmp[:, 7], c1, tmp[:, 4])
                mac(y[:, 15], tmp[:, 7], c1, tmp[:, 4], ALU.subtract)
                mac(y[:, 11], tmp[:, 6], c1, tmp[:, 5])
                n = mac(y[:, 13], tmp[:, 6], c1, tmp[:, 5], ALU.subtract)
                after(n)
                V.engine_nop().then_inc(y_ready, 1)

            def group(g):
                for j in range(XB):
                    w = 2 * P * min(2, ND - 2 * j)
                    dve.wait_ge(x_head, XB * g + j + 1)
                    V.tensor_tensor(X[:, 1, 2 * j:2 * j + 2].rearrange("p d r c -> p (d r c)")[:, 0:w],
                                    ps[:, (USES * g + j) % BANKS, 0:w],
                                    f32(X[:, 0, 2 * j:2 * j + 2]).rearrange("p d r c -> p (d r c)")[:, 0:w],
                                    ALU.subtract).then_inc(x_tail, 1)
                o = out[:, 0].rearrange("p (c d) -> p d c", d=A)
                if g:
                    dve.wait_ge(stored, 16 * g)
                for q, (d, w) in enumerate(DS):
                    imag = ps[:, (USES * g + XB + 2 * q + 1) % BANKS, 0:w * P].rearrange("p (d c) -> p d c", c=P)
                    re = real[:, (3 * g + q) % 2, 0:w * P].rearrange("p (d c) -> p d c", c=P)
                    dve.wait_ge(real_done, 3 * g + q + 1)
                    ins = V.scalar_tensor_tensor(out=o[:, d:d + w], in0=imag, scalar=ORTHO, in1=re,
                                                 op0=ALU.mult, op1=ALU.add)
                    f = max(d, 1)
                    if d + w <= ND - 1:
                        a, b = A - f, A - (d + w)
                        ins = V.scalar_tensor_tensor(out=o[:, a:b:-1, ::-1], in0=imag[:, f - d:], scalar=-ORTHO,
                                                     in1=re[:, f - d:], op0=ALU.mult, op1=ALU.add)
                    ins.then_inc(mirror_done, 1)

            dft16(0)
            dft16(1)
            for g in range(FNET_GROUPS):
                group(g)

        @block.scalar
        def _(act):
            act.wait_ge(tab_in, 32)
            nc.scalar.activation(ctab[:, 0], craw[:, :], ACT.Copy).then_inc(tab_head, 1)
            nc.scalar.activation(tab[:, 0], traw[:, :], ACT.Copy).then_inc(tab_head, 1)

            def heads(h):
                for e in range(2):
                    act.wait_ge(y_ready, 2 * h + e + 1)
                    if h:
                        act.wait_ge(x_mm, XB * GPC * h)
                    nc.scalar.activation(Y[:, 0, e::2], ub[:, h, e::2], ACT.Copy).then_inc(y_head, 1)

            def group(g):
                for j in range(XB):
                    w = 2 * P * min(2, ND - 2 * j)
                    act.wait_ge(x_mm, XB * g + j + 1)
                    if g:
                        act.wait_ge(out_mm, 3 * g)
                    nc.scalar.activation(X[:, 0, 2 * j:2 * j + 2].rearrange("p d r c -> p (d r c)")[:, 0:w],
                                         ps[:, (USES * g + j) % BANKS, 0:w], ACT.Copy).then_inc(x_head, 1)
                for q, (d, w) in enumerate(DS):
                    n = 3 * g + q
                    act.wait_ge(out_mm, n + 1)
                    if n >= 2:
                        act.wait_ge(mirror_done, n - 1)
                    nc.scalar.activation(real[:, n % 2, 0:w * P], ps[:, (USES * g + XB + 2 * q) % BANKS, 0:w * P],
                                         ACT.Copy, scale=ORTHO).then_inc(real_done, 1)

            heads(0)
            for g in range(FNET_GROUPS):
                if g == 1:
                    heads(1)
                group(g)

        @block.tensor
        def _(pe):
            def claim(n):
                if n < BANKS:
                    return
                g, j = divmod(n - BANKS, USES)
                if j < XB:
                    pe.wait_ge(x_tail, XB * g + j + 1)
                else:
                    pe.wait_ge(mirror_done, 3 * g + (j - XB) // 2 + 1)

            for g in range(FNET_GROUPS):
                h, c0 = g // GPC, (g % GPC) * P
                pe.wait_ge(tab_tail, 2)
                pe.wait_ge(y_tail, 2 * h + 2)
                for j in range(XB):
                    n = USES * g + j
                    claim(n)
                    for d in range(2 * j, min(2 * j + 2, ND)):
                        parts = [d] if d in (0, 8) else [d, 8 + d]
                        mms = [(i, a, b) for i in parts for a, b in SPLIT]
                        for q, (i, a, b) in enumerate(mms):
                            last = nc.tensor.matmul(ps[:, n % BANKS, (d % 2) * 256:(d % 2) * 256 + 256],
                                                    Y[:, a, i, c0:c0 + P], tab[:, b, i],
                                                    start=(q == 0), stop=(q == len(mms) - 1))
                    last.then_inc(x_mm, 1)
                pe.wait_ge(x_tail, XB * (g + 1))
                for q, (d, w) in enumerate(DS):
                    for r in range(2):
                        n = USES * g + XB + 2 * q + r
                        claim(n)
                        for i, (a, b) in enumerate(SPLIT):
                            last = nc.tensor.matmul(ps[:, n % BANKS, 0:w * P], ctab[:, a, r], X[:, b, d:d + w, r],
                                                    start=(i == 0), stop=(i == 2))
                    last.then_inc(out_mm, 1)


def fourier_tables():
    A, N = SEQ // P, SEQ
    b, c = np.arange(P)[:, None], np.arange(P)[None, :]
    pos = np.zeros((P, A, 2 * P), np.float64)
    for d in range(A // 2 + 1):
        th = 2 * np.pi * ((b * (A * c + d)) % N) / N
        pos[:, d] = np.concatenate([np.cos(th), -np.sin(th)], 1)
        if 0 < d < 8:
            sign = 1.0 if d == 6 else -1.0
            pos[:, 8 + d] = sign * np.concatenate([np.sin(th), np.cos(th)], 1)
    th = 2 * np.pi * ((b * c) % FNET_DIM) / FNET_DIM
    chan = np.stack([np.cos(th), np.sin(th)], 1)
    return pos.astype(np.float32), chan.astype(np.float32)


ROWS = SEQ // GRID_W
KR, KC = 16, 32
TI, TJ = ROWS // QR, GRID_W // QC
ROW0 = [min(max(QR * i - ROW_WIN // 2, 0), ROWS - KR) for i in range(TI)]
COL0 = [min(max(QC * j - COL_WIN // 2, 0), GRID_W - KC) for j in range(TJ)]
KIND = [0, 1, 1, 2]
KINDS = 3
REL_R, REL_C = 31, 64
PAD_R, PAD_C = 8, 16
BASE_R = [ROW0[i] - QR * i + ROW_WIN - 1 + PAD_R for i in (0, 1, 3)]
BASE_C = [COL0[j] - QC * j + COL_WIN - 1 + PAD_C for j in (0, 1, 3)]
RPB_R, RPB_C = 2 * ROW_WIN - 1, 2 * COL_WIN - 1
NEG = -1.0e30


def window_mask():
    out = np.full((KINDS * KINDS, QR, QC, KR, KC), NEG, np.float32)
    for a, i in enumerate((0, 1, 3)):
        for b, j in enumerate((0, 1, 3)):
            r = QR * i + np.arange(QR)[::-1]
            c = QC * j + np.arange(QC)
            r0 = np.clip(r - ROW_WIN // 2, 0, ROWS - ROW_WIN)[:, None]
            c0 = np.clip(c - COL_WIN // 2, 0, GRID_W - COL_WIN)[:, None]
            kr = ROW0[i] + np.arange(KR)[None, :]
            kc = COL0[j] + np.arange(KC)[None, :]
            rin = (kr >= r0) & (kr < r0 + ROW_WIN)
            cin = (kc >= c0) & (kc < c0 + COL_WIN)
            out[a * KINDS + b][rin[:, None, :, None] & cin[None, :, None, :]] = 0.0
    return out.reshape(KINDS * KINDS, P, KR * KC).transpose(1, 0, 2).copy()


def bias_phase(nc, rpb, padded, shifted):
    with ExitStack() as ctx:
        m = Pool(nc, ctx, "bt")
        zero = m.sb("zero", [REL_R * 4, P])
        zeroed, filled, placed, shifted_done = (m.sem(x) for x in ("zeroed", "filled", "placed", "shifted_done"))
        block = ctx.enter_context(nc.Block())

        @block.vector
        def _(dve):
            nc.vector.memset(zero[:, :], 0.0).then_inc(zeroed, 1)

        @block.sync
        def _(sp):
            sp.wait_ge(zeroed, 1)
            sp.dma_start(padded.rearrange("h r (x c) -> (h r x) c", x=1).rearrange("(p y) c -> p (y c)", y=2),
                         zero[:, :]).then_inc(filled, 16)
            sp.wait_ge(filled, 16)
            sp.dma_start(padded[:, PAD_R:PAD_R + RPB_R, PAD_C:PAD_C + RPB_C], rpb).then_inc(placed, 16)
            sp.wait_ge(placed, 16)
            for j in range(KINDS):
                for c in range(QC):
                    sp.dma_start(shifted[j, :, c], padded[:, :, BASE_C[j] - c:BASE_C[j] - c + KC]
                                 ).then_inc(shifted_done, 16)
            sp.wait_ge(shifted_done, 16 * KINDS * QC)


def attention_phase(nc, qT, kT, v, shifted, mask, eye, atT_out):
    H2 = 2 * HEAD_DIM
    KT = KR * KC // P
    VG = ROWS // 4
    TILES = TI * TJ
    N = HEADS * TILES
    NB = KINDS * KINDS
    SB, PTB, OB, TB = (0, 1, 2), (3, 4), (5, 6), 7
    with ExitStack() as ctx:
        m = Pool(nc, ctx, "at")
        qraw = m.sb("qraw", [P, SEQ])
        kraw = m.sb("kraw", [P, SEQ])
        vraw = m.sb("vraw", [P, VG * TJ, HEAD_DIM])
        qs = m.sb("qs", [P, 2, SEQ], F32R)
        kh = m.sb("kh", [P, 2, ROWS, GRID_W], F32R)
        kl = m.sb("kl", [P, 2, ROWS, GRID_W], F32R)
        vs = m.sb("vs", [P, 2, VG * TJ, H2], F32R)
        bias = m.sb("bias", [P, 2, NB, KR * KC])
        window = m.sb("window", [P, NB, KR * KC])
        neg = m.sb("neg", [P, 3, KR * KC])
        prob = m.sb("prob", [P, 3, KR * KC])
        pT = m.sb("pT", [P, 2, 2, KT, P], F32R)
        o = m.sb("o", [P, 2, TILES, H2])
        otail = m.sb("otail", [P, 2, HEAD_DIM])
        atT = m.sb("atT", [P, ROWS, GRID_W])
        ident = m.sb("ident", [P, P])
        negmax = m.sb("negmax", [P, N])
        total = m.sb("total", [P, N])
        inverse = m.sb("inverse", [P, N])
        ps = m.banks()

        const_in = m.sem("const_in")
        qk_in, v_in, bias_in = m.sem("qk_in"), m.sem("v_in"), m.sems("bias_in", 2)
        qk_head, qk_tail, v_head, v_tail, bias_ready = (
            m.sem(x) for x in ("qk_head", "qk_tail", "v_head", "v_tail", "bias_ready"))
        s_mm, s_red, p_exp, pT_mm, pT_head, pT_tail, o_mm, inverted, o_copied, o_merged = (
            m.sem(x) for x in ("s_mm", "s_red", "p_exp", "pT_mm", "pT_head", "pT_tail", "o_mm",
                               "inverted", "o_copied", "o_merged"))
        turned, evac, stored = m.sem("turned"), m.sem("evac"), m.sem("stored")

        def where(n):
            h, t = divmod(n, TILES)
            return h, t, t // TJ, t % TJ

        def turn_at(n):
            pair, t = divmod(n, 2 * TILES)
            if pair and t in (3, 5, 7, 9):
                return pair - 1, (t - 3) // 2
            return None

        block = ctx.enter_context(nc.Block())

        @block.sync
        def _(sp):
            sp.dma_start(ident[:, :], eye).then_inc(const_in, 16)

            def load(h):
                if h:
                    sp.wait_ge(qk_tail, 2 * h)
                for half in range(2):
                    for dst, src in ((qraw, qT), (kraw, kT)):
                        sp.dma_start(dst[half * HEAD_DIM:(half + 1) * HEAD_DIM, :],
                                     src[h * HEAD_DIM:(h + 1) * HEAD_DIM, :]).then_inc(qk_in, 16)
                if h >= 2:
                    sp.wait_ge(s_red, TILES * (h - 1))
                for i in range(KINDS):
                    for j in range(KINDS):
                        rows = shifted[j, h]
                        src = bass.AP(rows.tensor, rows.offset + (BASE_R[i] - (QR - 1)) * KC,
                                      [[KC, QR], [REL_R * KC, QC], [1, KR * KC]])
                        sp.dma_start(bias[:, h % 2, i * KINDS + j], src).then_inc(bias_in[h % 2], 16)
                if h == 0:
                    sp.dma_start(window[:, :], mask).then_inc(const_in, 16)
                if h:
                    sp.wait_ge(v_tail, h)
                vv = v.rearrange("(g r c) f -> r c g f", r=4, c=GRID_W)
                for r in range(4):
                    for j in range(TJ):
                        sp.dma_start(vraw[r * KC:(r + 1) * KC, j::TJ],
                                     vv[r, COL0[j]:COL0[j] + KC, :, h * HEAD_DIM:(h + 1) * HEAD_DIM]
                                     ).then_inc(v_in, 16)

            def store(pair):
                sp.wait_ge(evac, 4 * (pair + 1))
                sp.dma_start(atT_out[pair * P:(pair + 1) * P, :], atT[:, :]).then_inc(stored, 16)

            for h in range(HEADS):
                load(h)
                if h >= 4 and h % 2 == 0:
                    store((h - 4) // 2)
            for pair in range((HEADS - 3) // 2, HEADS // 2):
                store(pair)
            sp.wait_ge(stored, 16 * (HEADS // 2))

        @block.gpsimd
        def _(pool):
            G = nc.gpsimd
            for h in range(HEADS):
                s = h % 2
                pool.wait_ge(qk_head, 2 * h + 1)
                up = slice(HEAD_DIM, P)
                if h:
                    pool.wait_ge(v_tail, h)
                G.tensor_tensor(qs[up, s], qraw[up], f32(qs[up, s]), ALU.subtract).then_inc(qk_tail, 1)
                pool.wait_ge(qk_head, 2 * h + 2)
                pool.wait_ge(qk_tail, 2 * h + 1)
                G.tensor_tensor(kl[:, s], kraw.rearrange("p (r c) -> p r c", c=GRID_W), f32(kh[:, s]),
                                ALU.subtract).then_inc(qk_tail, 1)
                if h == 0:
                    pool.wait_ge(const_in, 32)
                pool.wait_ge(bias_in[s], 16 * NB * (h // 2 + 1))
                G.tensor_tensor(bias[:, s], bias[:, s], window[:, :], ALU.add).then_inc(bias_ready, 1)
                pool.wait_ge(v_head, h + 1)
                G.tensor_tensor(vs[:, s, :, HEAD_DIM:], vraw[:, :], f32(vs[:, s, :, 0:HEAD_DIM]),
                                ALU.subtract).then_inc(v_tail, 1)

        @block.vector
        def _(dve):
            V = nc.vector

            def qk_heads(h, part):
                s = h % 2
                dve.wait_ge(qk_in, 64 * (h + 1))
                if h >= 2:
                    dve.wait_ge(s_mm, TILES * (h - 1))
                if part == 0:
                    V.tensor_copy(qs[:, s], qraw[:, :]).then_inc(qk_head, 1)
                else:
                    V.tensor_copy(kh[:, s], kraw.rearrange("p (r c) -> p r c", c=GRID_W)).then_inc(qk_head, 1)

            def reduce(n):
                h, t, i, j = where(n)
                dve.wait_ge(s_mm, n + 1)
                if t == 0:
                    dve.wait_ge(bias_ready, h + 1)
                if n >= 3:
                    dve.wait_ge(p_exp, n - 2)
                V.tensor_tensor_reduce(out=neg[:, n % 3], in0=ps[:, SB[n % 3]],
                                       in1=bias[:, h % 2, KIND[i] * KINDS + KIND[j]], scale=-1.0, scalar=3.0e38,
                                       op0=ALU.add, op1=ALU.min, accum_out=negmax[:, n:n + 1]).then_inc(s_red, 1)

            def tail(n):
                dve.wait_ge(pT_head, n + 1)
                V.tensor_tensor(pT[:, n % 2, 1], ps[:, PTB[n % 2]].rearrange("p (k q) -> p k q", k=KT),
                                f32(pT[:, n % 2, 0]), ALU.subtract).then_inc(pT_tail, 1)

            def merge(n):
                h, t, _, _ = where(n)
                dve.wait_ge(o_copied, n + 1)
                pair = h // 2
                if pair >= 2 and h % 2 == 0 and t == 0:
                    dve.wait_ge(turned, 4 * (pair - 1))
                V.scalar_tensor_tensor(out=o[:, pair % 2, t, (h % 2) * HEAD_DIM:(h % 2 + 1) * HEAD_DIM],
                                       in0=ps[:, OB[n % 2], 0:HEAD_DIM], scalar=inverse[:, n:n + 1],
                                       in1=otail[:, n % 2], op0=ALU.mult, op1=ALU.add).then_inc(o_merged, 1)

            def invert(n):
                dve.wait_ge(p_exp, n + 1)
                V.reciprocal(inverse[:, n:n + 1], total[:, n:n + 1]).then_inc(inverted, 1)

            qk_heads(0, 0)
            qk_heads(0, 1)
            for n in range(-2, N):
                h, t, _, _ = where(max(n, 0))
                if n + 2 < N:
                    reduce(n + 2)
                if 0 <= n + 1 < N:
                    tail(n + 1)
                    invert(n + 1)
                if n >= 0:
                    merge(n)
                    if h + 1 < HEADS and t in (3, 5):
                        qk_heads(h + 1, (t - 3) // 2)

        @block.scalar
        def _(act):
            def v_heads(h):
                act.wait_ge(v_in, 16 * 16 * (h + 1))
                if h >= 2:
                    act.wait_ge(o_mm, TILES * (h - 1))
                nc.scalar.activation(vs[:, h % 2, :, 0:HEAD_DIM], vraw[:, :], ACT.Copy).then_inc(v_head, 1)

            def exp(n):
                act.wait_ge(s_red, n + 1)
                if n >= 3:
                    act.wait_ge(pT_mm, n - 2)
                nc.scalar.activation(prob[:, n % 3], neg[:, n % 3], ACT.Exp, scale=-1.0, bias=negmax[:, n:n + 1],
                                     accum_out=total[:, n:n + 1]).then_inc(p_exp, 1)

            def head(n):
                act.wait_ge(pT_mm, n + 1)
                if n >= 2:
                    act.wait_ge(o_mm, n - 1)
                nc.scalar.activation(pT[:, n % 2, 0], ps[:, PTB[n % 2]].rearrange("p (k q) -> p k q", k=KT),
                                     ACT.Copy).then_inc(pT_head, 1)

            def copy(n):
                act.wait_ge(o_mm, n + 1)
                act.wait_ge(inverted, n + 1)
                if n >= 2:
                    act.wait_ge(o_merged, n - 1)
                nc.scalar.activation(otail[:, n % 2], ps[:, OB[n % 2], HEAD_DIM:H2], ACT.Copy,
                                     scale=inverse[:, n:n + 1]).then_inc(o_copied, 1)

            def turn(pair, i):
                act.wait_ge(turned, 4 * pair + i + 1)
                if pair and i == 0:
                    act.wait_ge(stored, 16 * pair)
                nc.scalar.activation(
                    atT[:, i * QR:(i + 1) * QR].rearrange("p b (j c) -> p j b c", c=QC),
                    ps[:, TB].rearrange("p (j b c) -> p j b c", b=QR, c=QC)[:, :, ::-1], ACT.Copy).then_inc(evac, 1)

            for n in range(-2, N):
                h, t, _, _ = where(max(n, 0))
                if n + 2 < N:
                    exp(n + 2)
                if n == -2:
                    v_heads(0)
                if 0 <= n + 1 < N:
                    head(n + 1)
                if n >= 0:
                    copy(n)
                    if turn_at(n):
                        turn(*turn_at(n))
                    if h + 1 < HEADS and t == 7:
                        v_heads(h + 1)
            for i in range(TI):
                turn(HEADS // 2 - 1, i)

        @block.tensor
        def _(pe):
            def scores(n):
                h, t, i, j = where(n)
                if t == 0:
                    pe.wait_ge(qk_tail, 2 * h + 2)
                if n >= 3:
                    pe.wait_ge(s_red, n - 2)
                q = qs[:, h % 2, t * P:(t + 1) * P]
                for k in (kh, kl):
                    last = nc.tensor.matmul(ps[:, SB[n % 3]], q,
                                            k[:, h % 2, ROW0[i]:ROW0[i] + KR, COL0[j]:COL0[j] + KC],
                                            start=(k is kh), stop=(k is kl))
                last.then_inc(s_mm, 1)

            def transpose(n):
                pe.wait_ge(p_exp, n + 1)
                if n >= 2:
                    pe.wait_ge(pT_tail, n - 1)
                for k in range(KT):
                    last = nc.tensor.transpose(ps[:, PTB[n % 2], k * P:(k + 1) * P],
                                               prob[:, n % 3, k * P:(k + 1) * P], ident[:, :])
                last.then_inc(pT_mm, 1)

            def values(n):
                h, t, i, j = where(n)
                pe.wait_ge(pT_tail, n + 1)
                if t == 0:
                    pe.wait_ge(v_tail, h + 1)
                if n >= 2:
                    pe.wait_ge(o_merged, n - 1)
                for k in range(KT):
                    for part in range(2):
                        last = nc.tensor.matmul(ps[:, OB[n % 2], 0:H2], pT[:, n % 2, part, k],
                                                vs[:, h % 2, (ROW0[i] // 4 + k) * TJ + j],
                                                start=(k == 0 and part == 0), stop=(k == KT - 1 and part == 1))
                last.then_inc(o_mm, 1)

            def turn(pair, i):
                pe.wait_ge(o_merged, 2 * TILES * (pair + 1))
                if pair or i:
                    pe.wait_ge(evac, 4 * pair + i)
                for j in range(TJ):
                    last = nc.tensor.transpose(ps[:, TB, j * P:(j + 1) * P], o[:, pair % 2, i * TJ + j], ident[:, :])
                last.then_inc(turned, 1)

            pe.wait_ge(const_in, 16)
            for n in range(-2, N):
                if n + 2 < N:
                    scores(n + 2)
                if 0 <= n + 1 < N:
                    transpose(n + 1)
                if n >= 0:
                    values(n)
                    if turn_at(n):
                        turn(*turn_at(n))
            for i in range(TI):
                turn(HEADS // 2 - 1, i)


def at_least(engine, sem, value):
    if value > 0:
        engine.wait_ge(sem, value)


def mixer_output_phase(nc, x, fnT, atT, gT, w_mix, w_out, norm_g, eye, x2_out, hT_out):
    KA = (FNET_W + NA_W) // P
    HALF = D // 2
    SPH = HALF // P
    with ExitStack() as ctx:
        m = Pool(nc, ctx, "mo")
        araw = m.sb("araw", [P, 4, BLK])
        act_s = m.sb("act", [P, 2, KA, BLK], F32R)
        mixed = m.sb("mixed", [P, 2, KD, BLK], F32R)
        w = m.sb("w", [P, 2, 2, KA, P], F32R)
        wo = m.sb("wo", [P, 2, KD, KD, P], F32R)
        wraw = m.sb("wraw", [P, 2, KD, P])
        gate = m.sb("gate", [P, 2, 2, BLK])
        prod = m.sb("prod", [P, 2, BLK])
        mix = m.sb("mix", [P, 2, BLK])
        xt = m.sb("xt", [P, 3, D])
        h2 = m.sb("h2", [P, 2, D])
        turned_sb = m.sb("turned", [P, 1, KD, P])
        square = m.sb("square", [P, D], BF16)
        ident = m.sb("ident", [P, P])
        gain = m.sb("gain", [P, KD])
        sumsq, mean, root, rstd, corr, scale = (
            m.sb(s, [P, NTOK]) for s in ("sumsq", "mean", "root", "rstd", "corr", "scale"))
        ps = m.banks()

        const_in, a_in, w_in_raw, g_in, x_in = (
            m.sem("const_in"), m.sems("a_in", 4), m.sems("w_in", 2), m.sems("g_in", 2), m.sems("x_in", 3))
        a_head, a_tail, w_head, w_tail = (m.sem(s) for s in ("a_head", "a_tail", "w_head", "w_tail"))
        branch_mm, step, multiplied, mix_done, mix_head, mix_tail = (
            m.sem(s) for s in ("branch_mm", "step", "multiplied", "mix_done", "mix_head", "mix_tail"))
        out_mm, x2_done, sumsq_done, mean_done, root_done, h2_done = (
            m.sem(s) for s in ("out_mm", "x2_done", "sumsq_done", "mean_done", "root_done", "h2_done"))
        turned, evac = m.sem("turned_mm"), m.sem("evac")
        x2_stored, hT_stored = m.sems("x2_stored", 3), m.sem("hT_stored")

        order = [("mix", 0)]
        for b in range(NBLK):
            for s in range(KD):
                if s < KD - 1 or b < NBLK - 1:
                    order.append(("mix", (s + 1) % KD))
                order.append(("out", s))
        def w_index(b, kind, s):
            if kind == "mix":
                return 16 * b + (2 * s - 1 if s else (0 if b == 0 else -2))
            last = b == NBLK - 1 and s == KD - 1
            return 16 * b + 2 * s + (1 if last else 2)

        block = ctx.enter_context(nc.Block())

        @block.sync
        def _(sp):
            sp.dma_start(ident[:, :], eye).then_inc(const_in, 16)
            sp.dma_start(gain[:, :], norm_g).then_inc(const_in, 16)
            count = [0]

            def load_w():
                n = count[0]
                count[0] += 1
                at_least(sp, w_tail, n - 1)
                kind, t = order[n]
                sp.dma_start(wraw[:, n % 2], (w_mix if kind == "mix" else w_out)[t]).then_inc(w_in_raw[n % 2], 16)

            def load_a(b, k):
                n = b * KA + k
                at_least(sp, a_tail, n - 3)
                src = fnT if k < KA // 2 else atT
                r = (k % (KA // 2)) * P
                sp.dma_start(araw[:, n % 4], src[r:r + P, b * BLK:(b + 1) * BLK]).then_inc(a_in[n % 4], 16)

            for k in range(4):
                load_a(0, k)
            load_w()
            for k in range(4, KA):
                load_a(0, k)
            for b in range(NBLK):
                for s in range(KD):
                    n = b * KD + s
                    at_least(sp, mix_done, n - 1)
                    for branch in range(2):
                        r = branch * D + s * P
                        sp.dma_start(gate[:, n % 2, branch], gT[r:r + P, b * BLK:(b + 1) * BLK]
                                     ).then_inc(g_in[n % 2], 16)
                    if s < KD - 1 or b < NBLK - 1:
                        load_w()
                    load_w()
                for t in range(TPB):
                    n = b * TPB + t
                    at_least(sp, h2_done, n - 2)
                    if n >= 3:
                        sp.wait_ge(x2_stored[n % 3], 16 * (n // 3))
                    sp.dma_start(xt[:, n % 3], x[n * P:(n + 1) * P, :]).then_inc(x_in[n % 3], 16)
                    if b < NBLK - 1:
                        load_a(b + 1, 2 * t)
                        load_a(b + 1, 2 * t + 1)

        @block.gpsimd
        def _(pool):
            count = [0]

            def w_tails(number):
                for _ in range(number):
                    n = count[0]
                    count[0] += 1
                    kind, t = order[n]
                    pool.wait_ge(w_head, n + 1)
                    dst = w[:, :, t % 2] if kind == "mix" else wo[:, :, :, t]
                    nc.gpsimd.tensor_tensor(dst[:, 1], wraw[:, n % 2], f32(dst[:, 0]), ALU.subtract).then_inc(w_tail, 1)

            def a_tails(b, k):
                n = b * KA + k
                pool.wait_ge(a_head, n + 1)
                nc.gpsimd.tensor_tensor(act_s[:, 1, k], araw[:, n % 4], f32(act_s[:, 0, k]),
                                        ALU.subtract).then_inc(a_tail, 1)

            for k in range(KA):
                a_tails(0, k)
            w_tails(1)
            for b in range(NBLK):
                for s in range(KD):
                    w_tails(2 if s < KD - 1 or b < NBLK - 1 else 1)
                if b < NBLK - 1:
                    for k in range(KA):
                        a_tails(b + 1, k)

        @block.vector
        def _(dve):
            V = nc.vector
            count, steps = [0], [0]

            def after(ins):
                steps[0] += 1
                ins.then_inc(step, 1)
                dve.wait_ge(step, steps[0])

            def w_heads(b, s, number):
                for _ in range(number):
                    n = count[0]
                    count[0] += 1
                    kind, t = order[n]
                    dve.wait_ge(w_in_raw[n % 2], 16 * (n // 2 + 1))
                    if kind == "mix":
                        at_least(dve, branch_mm, 2 * (b * KD + s))
                        dst = w[:, 0, t % 2]
                    else:
                        at_least(dve, out_mm, 2 * TPB * b)
                        dst = wo[:, 0, :, t]
                    V.tensor_copy(dst, wraw[:, n % 2]).then_inc(w_head, 1)

            def a_heads(b, k):
                n = b * KA + k
                dve.wait_ge(a_in[n % 4], 16 * (n // 4 + 1))
                at_least(dve, branch_mm, 2 * KD * b)
                V.tensor_copy(act_s[:, 0, k], araw[:, n % 4]).then_inc(a_head, 1)

            def gated(b, s):
                n = b * KD + s
                dve.wait_ge(g_in[n % 2], 32 * (n // 2 + 1))
                at_least(dve, mix_done, n)
                for branch in range(2):
                    dve.wait_ge(branch_mm, 2 * n + branch + 1)
                    V.tensor_tensor(prod[:, branch], ps[:, 2 * (n % 2) + branch], gate[:, n % 2, branch],
                                    ALU.mult).then_inc(multiplied, 1)
                dve.wait_ge(multiplied, 2 * n + 2)
                at_least(dve, mix_tail, n - 1)
                V.tensor_tensor(mix[:, n % 2], prod[:, 0], prod[:, 1], ALU.add).then_inc(mix_done, 1)

            def mix_tails(n):
                dve.wait_ge(mix_head, n + 1)
                V.tensor_tensor(mixed[:, 1, n % KD], mix[:, n % 2], f32(mixed[:, 0, n % KD]),
                                ALU.subtract).then_inc(mix_tail, 1)

            def finish(b, t):
                n = b * TPB + t
                c = slice(n, n + 1)
                dve.wait_ge(x_in[n % 3], 16 * (n // 3 + 1))
                for half in range(2):
                    dve.wait_ge(out_mm, 2 * n + half + 1)
                    part = xt[:, n % 3, half * HALF:(half + 1) * HALF]
                    V.tensor_tensor(part, ps[:, 4 + half], part, ALU.add).then_inc(x2_done, 1)
                dve.wait_ge(sumsq_done, n + 1)
                V.tensor_scalar(mean[:, c], sumsq[:, c], 1.0 / D, EPS, ALU.mult, ALU.add).then_inc(mean_done, 1)
                dve.wait_ge(root_done, n + 1)
                after(V.reciprocal(rstd[:, c], root[:, c]))
                after(V.tensor_scalar(corr[:, c], rstd[:, c], rstd[:, c], mean[:, c], ALU.mult, ALU.mult))
                after(V.tensor_scalar(scale[:, c], corr[:, c], -0.5, 1.5, ALU.mult, ALU.add))
                after(V.tensor_tensor(rstd[:, c], rstd[:, c], scale[:, c], ALU.mult))
                at_least(dve, turned, n - 1)
                V.tensor_scalar(h2[:, n % 2], xt[:, n % 3], rstd[:, c], None, ALU.mult).then_inc(h2_done, 1)

            for k in range(KA):
                a_heads(0, k)
            w_heads(0, 0, 1)
            for b in range(NBLK):
                for s in range(KD):
                    w_heads(b, s, 2 if s < KD - 1 or b < NBLK - 1 else 1)
                    gated(b, s)
                    if s:
                        mix_tails(b * KD + s - 1)
                mix_tails(b * KD + KD - 1)
                for t in range(TPB):
                    finish(b, t)
                    if b < NBLK - 1:
                        a_heads(b + 1, 2 * t)
                        a_heads(b + 1, 2 * t + 1)

        @block.scalar
        def _(act):
            act.wait_ge(const_in, 32)

            def mix_heads(n):
                act.wait_ge(mix_done, n + 1)
                if n >= KD:
                    act.wait_ge(out_mm, 2 * TPB * (n // KD))
                nc.scalar.activation(mixed[:, 0, n % KD], mix[:, n % 2], ACT.Copy).then_inc(mix_head, 1)

            def stats(n):
                act.wait_ge(x2_done, 2 * n + 2)
                at_least(act, sumsq_done, n)
                nc.scalar.activation(square[:, :], xt[:, n % 3], ACT.Square,
                                     accum_out=sumsq[:, n:n + 1]).then_inc(sumsq_done, 1)
                act.dma_start(x2_out[n * P:(n + 1) * P, :], xt[:, n % 3]).then_inc(x2_stored[n % 3], 16)
                act.wait_ge(mean_done, n + 1)
                nc.scalar.activation(root[:, n:n + 1], mean[:, n:n + 1], ACT.Sqrt).then_inc(root_done, 1)

            def spill(n):
                act.wait_ge(turned, n + 1)
                if n:
                    act.wait_ge(hT_stored, 16 * n)
                for k in range(KD):
                    nc.scalar.activation(turned_sb[:, 0, k], ps[:, 6 + k // 4, (k % 4) * P:(k % 4 + 1) * P], ACT.Copy,
                                         scale=gain[:, k:k + 1]).then_inc(evac, 1)
                act.wait_ge(evac, KD * (n + 1))
                act.dma_start(hT_out.rearrange("(k p) t -> p k t", p=P)[:, :, n * P:(n + 1) * P],
                              turned_sb[:, 0]).then_inc(hT_stored, 16)

            for b in range(NBLK):
                for s in range(KD):
                    mix_heads(b * KD + s)
                    if b and s == 1:
                        spill(b * TPB - 1)
                for t in range(TPB):
                    stats(b * TPB + t)
                    if t:
                        spill(b * TPB + t - 1)
            spill(NTOK - 1)
            for s in range(3):
                act.wait_ge(x2_stored[s], 16 * len(range(s, NTOK, 3)))
            act.wait_ge(hT_stored, 16 * NTOK)

        @block.tensor
        def _(pe):
            def branches(b, s):
                n = b * KD + s
                pe.wait_ge(w_tail, w_index(b, "mix", s) + 1)
                for branch in range(2):
                    at_least(pe, multiplied, 2 * (n - 2) + branch + 1)
                    ks = range(branch * KA // 2, (branch + 1) * KA // 2)
                    for k in ks:
                        if s == 0:
                            pe.wait_ge(a_tail, b * KA + k + 1)
                        for a, c in SPLIT:
                            last = nc.tensor.matmul(ps[:, 2 * (n % 2) + branch], w[:, a, s % 2, k], act_s[:, c, k],
                                                    start=(k == ks[0] and (a, c) == SPLIT[0]),
                                                    stop=(k == ks[-1] and (a, c) == SPLIT[-1]))
                    last.then_inc(branch_mm, 1)

            def output(b, t):
                n = b * TPB + t
                for half in range(2):
                    at_least(pe, x2_done, 2 * (n - 1) + half + 1)
                    if t == 0:
                        pe.wait_ge(w_tail, w_index(b, "out", (half + 1) * SPH - 1) + 1)
                    for k in range(KD):
                        if t == 0 and half == 0:
                            pe.wait_ge(mix_tail, b * KD + k + 1)
                        for a, c in SPLIT:
                            last = nc.tensor.matmul(ps[:, 4 + half], mixed[:, a, k, t * P:(t + 1) * P],
                                                    wo[:, c, k, half * SPH:(half + 1) * SPH],
                                                    start=(k == 0 and (a, c) == SPLIT[0]),
                                                    stop=(k == KD - 1 and (a, c) == SPLIT[-1]))
                    last.then_inc(out_mm, 1)

            def turn(n):
                pe.wait_ge(h2_done, n + 1)
                at_least(pe, evac, KD * n)
                for k in range(KD):
                    last = nc.tensor.transpose(ps[:, 6 + k // 4, (k % 4) * P:(k % 4 + 1) * P],
                                               h2[:, n % 2, k * P:(k + 1) * P], ident[:, :])
                last.then_inc(turned, 1)

            pe.wait_ge(const_in, 32)
            for b in range(NBLK):
                for s in range(KD):
                    branches(b, s)
                    if b and s == 1:
                        turn(b * TPB - 1)
                for t in range(TPB):
                    output(b, t)
                    if t:
                        turn(b * TPB + t - 1)
            turn(NTOK - 1)


def conv_ffn_phase(nc, x2, hT, w_up, w_down, conv, final_g, out):
    FK = D_FF // P
    UP = 2 * FK
    DOWN = FK
    PER = UP + DOWN
    ITER = 4
    HALF = D // 2
    W = BLK + 1
    LEAD = P - 1
    TAPS, EDGE, BODY = 0, 4, 6
    CHUNKS = [list(range(max(0, TPB * b - 1), TPB * b + TPB - 1 + (b == NBLK - 1))) for b in range(NBLK)]
    SLOTS = max(len(c) for c in CHUNKS)
    ACC = (4, 5, 6, 7, 0)
    BEFORE = [sum(len(c) for c in CHUNKS[:b]) for b in range(NBLK + 1)]

    def column(b, i):
        return i * P + (P if b == 0 else 0)

    with ExitStack() as ctx:
        m = Pool(nc, ctx, "ff")
        hid = m.sb("hid", [P, 2, FK, BLK + P], F32R)
        h = m.sb("h", [P, 2, KD, BLK], F32R)
        w = m.sb("w", [P, 2, 2, KD * P], F32R)
        wraw = m.sb("wraw", [P, 2, KD * P])
        hraw = m.sb("hraw", [P, 2, BLK])
        y = m.sb("y", [P, SLOTS, D])
        u = m.sb("u", [P, 2, BODY + BLK + 1])
        val = m.sb("val", [P, W])
        gate = m.sb("gate", [P, W])
        gain = m.sb("gain", [P, D])
        param = m.sb("param", [P, UP, BODY])
        square = m.sb("square", [P, D], BF16)
        sumsq, mean, root, rstd, corr, scale = (
            m.sb(s, [P, NTOK]) for s in ("sumsq", "mean", "root", "rstd", "corr", "scale"))
        ps = m.banks()

        const_in, h_in, w_in, y_in = m.sem("const_in"), m.sems("h_in", 2), m.sems("w_in", 2), m.sem("y_in")
        cleared, h_head, h_tail, w_head, w_tail = (
            m.sem(s) for s in ("cleared", "h_head", "h_tail", "w_head", "w_tail"))
        used = m.sem("used")
        copied, edges, conv_done, silu_done, prod_done, hid_head, hid_tail, step = (
            m.sem(s) for s in ("copied", "edges", "conv_done", "silu_done", "prod_done", "hid_head", "hid_tail", "step"))
        step_up = m.sem("step_up")
        shifted_head, shifted_tail = m.sem("shifted_head"), m.sem("shifted_tail")
        added, sumsq_done, mean_done, root_done, y_done, stored = (
            m.sem(s) for s in ("added", "sumsq_done", "mean_done", "root_done", "y_done", "stored"))

        def ge(engine, sem, base, i=0, per=0):
            if isinstance(i, int):
                at_least(engine, sem, base + per * i)
            else:
                engine.wait_ge(sem, i * per + base)

        def up_steps(engine, step_fn, b, extra=None):
            for j in range(ITER):
                step_fn(b, 0, j)
                if extra:
                    extra(b, j)
            with engine.Fori(1, UP // ITER - 1) as i:
                for j in range(ITER):
                    step_fn(b, i, j)
            for j in range(ITER):
                step_fn(b, UP // ITER - 1, j)

        block = ctx.enter_context(nc.Block())

        @block.sync
        def _(sp):
            sp.dma_start(param[:, :, TAPS:EDGE], conv).then_inc(const_in, 16)
            sp.dma_start(gain[:, :], bass.AP(final_g.tensor, final_g.offset, [[0, P], [1, D]])).then_inc(const_in, 16)

            def load_up(b, i, j):
                ge(sp, w_tail, PER * b + j - 1, i, ITER)
                if isinstance(i, int):
                    src = w_up[ITER * i + j]
                else:
                    src = w_up[bass.ds(i * ITER + j, 1)].rearrange("o p c -> (o p) c")
                sp.dma_start(wraw[:, j % 2], src).then_inc(w_in[j % 2], 16)

            def load_down(b, d):
                sp.wait_ge(w_tail, PER * b + UP + d - 1)
                sp.dma_start(wraw[:, d % 2], w_down[d]).then_inc(w_in[d % 2], 16)

            def load_h(b, k):
                n = b * KD + k
                at_least(sp, h_tail, n - 1)
                sp.dma_start(hraw[:, n % 2], hT[k * P:(k + 1) * P, b * BLK:(b + 1) * BLK]).then_inc(h_in[n % 2], 16)

            def load_y(b, i):
                t = CHUNKS[b][i]
                if b:
                    sp.wait_ge(stored, 16 * BEFORE[b])
                sp.dma_start(y[:, i], x2[t * P:(t + 1) * P, :]).then_inc(y_in, 16)

            def store(b, i):
                n = BEFORE[b] + i
                sp.wait_ge(y_done, n + 1)
                sp.dma_start(out[CHUNKS[b][i] * P:(CHUNKS[b][i] + 1) * P, :], y[:, i]).then_inc(stored, 16)

            for k in range(KD):
                load_h(0, k)
                if k in (1, 3):
                    load_up(0, 0, k // 2)
            for b in range(NBLK):
                load_up(b, 0, 2)
                load_up(b, 0, 3)
                with sp.Fori(1, UP // ITER) as i:
                    for j in range(ITER):
                        load_up(b, i, j)
                load_down(b, 0)
                if b:
                    for i in range(len(CHUNKS[b - 1])):
                        store(b - 1, i)
                for d in range(1, DOWN):
                    load_down(b, d)
                    if d == 2:
                        for i in range(len(CHUNKS[b])):
                            load_y(b, i)
                    if b < NBLK - 1 and 2 < d <= 2 + KD:
                        load_h(b + 1, d - 3)
                if b < NBLK - 1:
                    load_up(b + 1, 0, 0)
                    load_up(b + 1, 0, 1)
            for i in range(len(CHUNKS[-1])):
                store(NBLK - 1, i)
            sp.wait_ge(stored, 16 * NTOK)

        @block.gpsimd
        def _(pool):
            def w_tails(n, slot, i=0, per=0):
                ge(pool, w_head, n + 1, i, per)
                nc.gpsimd.tensor_tensor(w[:, 1, slot], wraw[:, slot], f32(w[:, 0, slot]), ALU.subtract).then_inc(w_tail, 1)

            def h_tails(b, k):
                n = b * KD + k
                pool.wait_ge(h_head, n + 1)
                nc.gpsimd.tensor_tensor(h[:, 1, k], hraw[:, n % 2], f32(h[:, 0, k]), ALU.subtract).then_inc(h_tail, 1)

            for k in range(KD):
                h_tails(0, k)
                if k in (3, 5):
                    w_tails((k - 3) // 2, (k - 3) // 2)
            for b in range(NBLK):
                w_tails(PER * b + 2, 0)
                w_tails(PER * b + 3, 1)
                with pool.Fori(1, UP // ITER) as i:
                    for j in range(ITER):
                        w_tails(PER * b + j, j % 2, i, ITER)
                for d in range(DOWN + 2 * (b < NBLK - 1)):
                    w_tails(PER * b + UP + d, d % 2)
                    if b < NBLK - 1 and 3 <= d < 3 + KD:
                        h_tails(b + 1, d - 3)

        @block.vector
        def _(dve):
            V = nc.vector
            steps = [0]

            def after(ins):
                steps[0] += 1
                ins.then_inc(step, 1)
                dve.wait_ge(step, steps[0])

            def w_heads(b, t, i=0, per=0):
                n = PER * b + t
                ge(dve, w_in[t % 2], 16 * (n // 2 + 1), i, 16 * per // 2)
                ge(dve, used, n - 1, i, per)
                V.tensor_copy(w[:, 0, t % 2], wraw[:, t % 2]).then_inc(w_head, 1)

            def h_heads(b, k):
                n = b * KD + k
                dve.wait_ge(h_in[n % 2], 16 * (n // 2 + 1))
                at_least(dve, used, PER * (b - 1) + UP if b else 0)
                V.tensor_copy(h[:, 0, k], hraw[:, n % 2]).then_inc(h_head, 1)

            def up_step(b, i, j):
                w_heads(b, j + 2, i, ITER)
                t = UP * b + j
                par = lambda: param[:, ITER * i + j] if isinstance(i, int) else (
                    param[:, bass.ds(i * ITER + j, 1)].rearrange("p o c -> p (o c)"))
                s = j % 2
                dst = (val, gate)[s]
                k = 2 * i + j // 2 if isinstance(i, int) else None
                hk = lambda part: hid[:, part, k, LEAD:] if k is not None else (
                    hid[:, part, bass.ds(i * 2 + j // 2, 1), LEAD:].rearrange("p o c -> p (o c)"))
                ge(dve, conv_done, t - 1, i, ITER)
                V.tensor_scalar(u[:, s, TAPS:BODY], par(), 1.0, None, ALU.mult).then_inc(edges, 1)
                ge(dve, copied, t + 1, i, ITER)
                ge(dve, edges, 2 * t + 1, i, 2 * ITER)
                V.tensor_scalar(par()[:, EDGE:], u[:, s, BODY + BLK - 2:BODY + BLK], 1.0, None, ALU.mult).then_inc(edges, 1)
                tap = lambda q: u[:, s, TAPS + q:TAPS + q + 1]
                ge(dve, prod_done, (t - 1) // 2 if s == 0 else (t + 1) // 2 - 1, i, ITER // 2)
                if s:
                    ge(dve, prod_done, (t - 1) // 2, i, ITER // 2)
                V.tensor_scalar(dst[:, :], u[:, s, EDGE + 1:EDGE + 1 + W], tap(1), tap(3), ALU.mult, ALU.add
                                ).then_inc(step_up, 1)
                ge(dve, step_up, 2 * t + 1, i, 2 * ITER)
                V.scalar_tensor_tensor(out=dst[:, :], in0=u[:, s, EDGE:EDGE + W], scalar=tap(0), in1=dst[:, :],
                                       op0=ALU.mult, op1=ALU.add).then_inc(step_up, 1)
                ge(dve, step_up, 2 * t + 2, i, 2 * ITER)
                ge(dve, edges, 2 * t + 2, i, 2 * ITER)
                V.scalar_tensor_tensor(out=dst[:, :], in0=u[:, s, EDGE + 2:EDGE + 2 + W], scalar=tap(2), in1=dst[:, :],
                                       op0=ALU.mult, op1=ALU.add).then_inc(conv_done, 1)
                if s:
                    p = (t - 1) // 2
                    ge(dve, silu_done, p + 1, i, ITER // 2)
                    V.tensor_tensor(val[:, :], val[:, :], gate[:, :], ALU.mult).then_inc(prod_done, 1)
                    ge(dve, prod_done, p + 1, i, ITER // 2)
                    V.tensor_scalar(hk(0), val[:, :], 1.0, None, ALU.mult).then_inc(hid_head, 1)
                    ge(dve, hid_head, p + 1, i, ITER // 2)
                    V.tensor_tensor(hk(1), val[:, :], f32(hk(0)), ALU.subtract).then_inc(hid_tail, 1)
                    ge(dve, hid_tail, p + 1, i, ITER // 2)

            def add(b, half):
                for i in range(len(CHUNKS[b])):
                    if half == 0:
                        dve.wait_ge(y_in, 16 * BEFORE[b + 1])
                    add_one(b, half, i)

            def add_one(b, half, i):
                dve.wait_ge(used, PER * b + UP + (half + 1) * (DOWN // 2))
                part = y[:, i, half * HALF:(half + 1) * HALF]
                V.tensor_tensor(part, ps[:, ACC[i]], part, ALU.add).then_inc(added, 1)

            def finish(b, i):
                n = BEFORE[b] + i
                c = slice(n, n + 1)
                add_one(b, 1, i)
                dve.wait_ge(sumsq_done, n + 1)
                V.tensor_scalar(mean[:, c], sumsq[:, c], 1.0 / D, EPS, ALU.mult, ALU.add).then_inc(mean_done, 1)
                dve.wait_ge(root_done, n + 1)
                after(V.reciprocal(rstd[:, c], root[:, c]))
                after(V.tensor_scalar(corr[:, c], rstd[:, c], rstd[:, c], mean[:, c], ALU.mult, ALU.mult))
                after(V.tensor_scalar(scale[:, c], corr[:, c], -0.5, 1.5, ALU.mult, ALU.add))
                after(V.tensor_tensor(rstd[:, c], rstd[:, c], scale[:, c], ALU.mult))
                V.scalar_tensor_tensor(out=y[:, i], in0=y[:, i], scalar=rstd[:, c], in1=gain[:, :],
                                       op0=ALU.mult, op1=ALU.mult).then_inc(y_done, 1)

            def extra(b, j):
                if b and j < len(CHUNKS[b - 1]):
                    finish(b - 1, j)

            V.memset(param[:, :, EDGE:BODY], 0.0).then_inc(cleared, 1)
            V.memset(hid[:, :, :, 0:LEAD].bitcast(F32), 0.0).then_inc(cleared, 1)
            V.memset(u[:, :, BODY + BLK:], 0.0).then_inc(cleared, 1)
            dve.wait_ge(cleared, 3)
            dve.wait_ge(const_in, 32)
            for k in range(KD):
                h_heads(0, k)
                if k in (3, 5):
                    w_heads(0, (k - 3) // 2)
            for b in range(NBLK):
                up_steps(dve, up_step, b, extra)
                for d in range(DOWN):
                    if d < DOWN - 2:
                        w_heads(b, UP + d + 2)
                    elif b < NBLK - 1:
                        w_heads(b + 1, d - (DOWN - 2))
                    if d == DOWN // 2 - 1:
                        add(b, 0)
                    if b < NBLK - 1 and 1 <= d < 1 + KD:
                        h_heads(b + 1, d - 1)
                if b < NBLK - 1:
                    dve.wait_ge(used, PER * (b + 1))
                    V.tensor_copy(hid[:, 0, :, 0:LEAD], f32(hid[:, 0, :, BLK:BLK + LEAD])).then_inc(shifted_head, 1)
                    dve.wait_ge(shifted_head, b + 1)
                    dve.wait_ge(shifted_tail, b + 1)
            for i in range(len(CHUNKS[-1])):
                finish(NBLK - 1, i)

        @block.scalar
        def _(act):
            def up_step(b, i, j):
                t = UP * b + j
                s = j % 2
                ge(act, used, PER * b + j + 1, i, ITER)
                ge(act, conv_done, t - 1, i, ITER)
                nc.scalar.activation(u[:, s, BODY:BODY + BLK], ps[:, j], ACT.Copy).then_inc(copied, 1)
                if s:
                    ge(act, conv_done, t + 1, i, ITER)
                    nc.scalar.activation(gate[:, :], gate[:, :], ACT.Silu).then_inc(silu_done, 1)

            def stats(b, i):
                n = BEFORE[b] + i
                act.wait_ge(added, BEFORE[b + 1] + n + 1)
                at_least(act, sumsq_done, n)
                nc.scalar.activation(square[:, :], y[:, i], ACT.Square, accum_out=sumsq[:, n:n + 1]).then_inc(sumsq_done, 1)
                act.wait_ge(mean_done, n + 1)
                nc.scalar.activation(root[:, n:n + 1], mean[:, n:n + 1], ACT.Sqrt).then_inc(root_done, 1)

            def extra(b, j):
                if b and j < len(CHUNKS[b - 1]):
                    stats(b - 1, j)

            for b in range(NBLK):
                up_steps(act, up_step, b, extra)
                if b < NBLK - 1:
                    act.wait_ge(used, PER * (b + 1))
                    act.wait_ge(hid_tail, FK * (b + 1))
                    nc.scalar.activation(hid[:, 1, :, 0:LEAD], f32(hid[:, 1, :, BLK:BLK + LEAD]), ACT.Copy).then_inc(shifted_tail, 1)
            for i in range(len(CHUNKS[-1])):
                stats(NBLK - 1, i)

        @block.tensor
        def _(pe):
            def up_step(b, i, j):
                t = UP * b + j
                ge(pe, w_tail, PER * b + j + 1, i, ITER)
                ge(pe, copied, t - 3, i, ITER)
                for k in range(KD):
                    if isinstance(i, int) and i == 0 and j == 0:
                        pe.wait_ge(h_tail, b * KD + k + 1)
                    for a, c in SPLIT:
                        last = nc.tensor.matmul(ps[:, j], w[:, a, j % 2, k * P:(k + 1) * P], h[:, c, k],
                                                start=(k == 0 and (a, c) == SPLIT[0]),
                                                stop=(k == KD - 1 and (a, c) == SPLIT[-1]))
                last.then_inc(used, 1)

            def down(b):
                for d in range(DOWN):
                    half, pair = divmod(d, DOWN // 2)
                    pe.wait_ge(w_tail, PER * b + UP + d + 1)
                    for q in range(2):
                        k = 2 * pair + q
                        if half == 0:
                            pe.wait_ge(hid_tail, FK * b + k + 1)
                            if b and d == 0 and q == 0:
                                pe.wait_ge(shifted_head, b)
                                pe.wait_ge(shifted_tail, b)
                        for i in range(len(CHUNKS[b])):
                            if pair == 0 and q == 0:
                                if half:
                                    pe.wait_ge(added, 2 * BEFORE[b] + i + 1)
                                elif b:
                                    pe.wait_ge(added, 2 * BEFORE[b])
                                if i == TPB:
                                    pe.wait_ge(copied, UP * (b + 1))
                            c0 = column(b, i)
                            for a, c in SPLIT:
                                last = nc.tensor.matmul(ps[:, ACC[i]], hid[:, a, k, c0:c0 + P],
                                                        w[:, c, d % 2, q * HALF:(q + 1) * HALF],
                                                        start=(k == 0 and (a, c) == SPLIT[0]),
                                                        stop=(k == FK - 1 and (a, c) == SPLIT[-1]))
                    last.then_inc(used, 1)

            for b in range(NBLK):
                up_steps(pe, up_step, b)
                down(b)


def encoder_layer(nc, x, w_in, norm1_g, b_gate, rpb, w_mix, w_out, norm2_g, w_up, w_down, conv, final_g,
                  pos_table, chan_table, mask, eye, out):
    def scratch(name, *shape):
        return nc.dram_tensor(name, shape, F32, kind="Internal").ap()

    u, v = scratch("u", SEQ, FNET_W), scratch("v", SEQ, NA_W)
    qT, kT = scratch("qT", NA_W, SEQ), scratch("kT", NA_W, SEQ)
    gT = scratch("gT", 2 * D, SEQ)
    fnT, atT = scratch("fnT", FNET_W, SEQ), scratch("atT", NA_W, SEQ)
    x2, hT = scratch("x2", SEQ, D), scratch("hT", D, SEQ)
    padded = scratch("padded", HEADS, REL_R, REL_C)
    shifted = scratch("shifted", KINDS, HEADS, QC, REL_R, KC)

    input_phase(nc, x, w_in, norm1_g, b_gate, eye, u, qT, v, kT, gT)
    fourier_phase(nc, u, pos_table, chan_table, fnT)
    bias_phase(nc, rpb, padded, shifted)
    attention_phase(nc, qT, kT, v, shifted, mask, eye, atT)
    mixer_output_phase(nc, x, fnT, atT, gT, w_mix, w_out, norm2_g, eye, x2, hT)
    conv_ffn_phase(nc, x2, hT, w_up, w_down, conv, final_g, out)


def column_tiles(w):
    return w.reshape(KD, P, -1, P).transpose(2, 1, 0, 3)


def kernel(x, norm1_g, w_in, b_gate, rpb, w_fa, w_nb, w_out, norm2_g, w_up, conv_w, conv_b, w_down, final_g):
    import concourse.bacc as _bacc
    from concourse.bass_utils import run_bass_kernel_spmd as _run

    x, norm1_g, w_in, b_gate, rpb, w_fa, w_nb, w_out, norm2_g, w_up, conv_w, conv_b, w_down, final_g = (
        np.asarray(a) for a in (x, norm1_g, w_in, b_gate, rpb, w_fa, w_nb, w_out, norm2_g, w_up, conv_w, conv_b,
                                w_down, final_g))
    pos, chan = fourier_tables()
    taps = np.concatenate([conv_w[0], conv_b], axis=0)
    layout = {
        "x": x.reshape(SEQ, D),
        "w_in": column_tiles(w_in[0]),
        "norm1_g": norm1_g[0].reshape(KD, P).T,
        "b_gate": b_gate[0].reshape(2 * KD, P).T,
        "rpb": rpb[0],
        "w_mix": column_tiles(np.concatenate([w_fa[0], w_nb[0]], axis=0)),
        "w_out": column_tiles(w_out[0]),
        "norm2_g": norm2_g[0].reshape(KD, P).T,
        "w_up": w_up[0].reshape(KD, P, 2, D_FF // P, P).transpose(3, 2, 1, 0, 4).reshape(2 * D_FF // P, P, D),
        "w_down": w_down[0].reshape(D_FF // (2 * P), 2, P, 2, D // 2).transpose(3, 0, 2, 1, 4).reshape(D_FF // P, P, D),
        "conv": taps.reshape(4, 2, D_FF // P, P).transpose(3, 2, 1, 0).reshape(P, 2 * D_FF // P, 4),
        "final_g": final_g,
        "pos_table": pos,
        "chan_table": chan,
        "mask": window_mask(),
        "eye": np.eye(P, dtype=np.float32),
    }
    nc = _bacc.Bacc("TRN2", target_bir_lowering=False, num_devices=1)
    arrays, args = {}, []
    for name, a in layout.items():
        arrays[f"in_{name}_dram"] = np.ascontiguousarray(a)
        args.append(nc.dram_tensor(f"in_{name}_dram", a.shape, F32, kind="ExternalInput").ap())
    args.append(nc.dram_tensor("out_0_dram", (SEQ, D), F32, kind="ExternalOutput").ap())
    encoder_layer(nc, *args)
    r = _run(nc, [arrays], core_ids=[0])
    return np.asarray(r.results[0]["out_0_dram"]).reshape(x.shape)
```

```python
from contextlib import ExitStack

import numpy as np

import concourse.bass as bass
from concourse import mybir

F32 = mybir.dt.float32
F32R = mybir.dt.float32r
BF16 = mybir.dt.bfloat16
ALU = mybir.AluOpType
ACT = mybir.ActivationFunctionType
AX = mybir.AxisListType

P = 128
D = 1024
SEQ = 2048
KD = D // P
NTOK = SEQ // P
BLK = 512
NBLK = SEQ // BLK
TPB = BLK // P
GRID_W = 64
FNET_GROUPS, FNET_DIM = 4, 128
FNET_W = FNET_GROUPS * FNET_DIM
HEADS, HEAD_DIM = 8, 64
NA_W = HEADS * HEAD_DIM
ROW_WIN, COL_WIN = 8, 16
D_FF = 2816
EPS = 1e-6
BANKS = 8
QR, QC = 8, 16


def f32(ap):
    return ap.bitcast(F32)


SPLIT = ((0, 0), (0, 1), (1, 0))


class Pool:

    def __init__(self, nc, ctx, tag):
        self.nc, self.ctx, self.tag = nc, ctx, tag

    def sb(self, name, shape, dt=F32):
        return self.ctx.enter_context(self.nc.sbuf_tensor(f"{self.tag}_{name}", shape, dt))

    def banks(self):
        return self.ctx.enter_context(self.nc.psum_tensor(f"{self.tag}_psum", [P, BANKS, BLK], F32))

    def sem(self, name):
        return self.ctx.enter_context(self.nc.semaphore(f"{self.tag}_{name}"))

    def sems(self, name, n):
        return [self.sem(f"{name}{i}") for i in range(n)]


def input_phase(nc, x, w_in, norm_g, b_gate, eye, u_out, qT_out, v_out, kT_out, gT_out):
    RAW, STAGES, XS = 2, 4, 2
    with ExitStack() as ctx:
        m = Pool(nc, ctx, "in")
        hT = m.sb("hT", [P, 2, KD, SEQ], F32R)
        w = m.sb("w", [P, 2, 6, KD, P], F32R)
        wraw = m.sb("wraw", [P, RAW, KD, P])
        stage = m.sb("stage", [P, STAGES, BLK])
        xt = m.sb("xt", [P, XS, D])
        square = m.sb("square", [P, D], BF16)
        ident = m.sb("ident", [P, P])
        gain = m.sb("gain", [P, D])
        gbias = m.sb("gbias", [P, 2 * KD])
        bias_now = m.sb("bias_now", [P, 2])
        sumsq = m.sb("sumsq", [P, NTOK])
        mean = m.sb("mean", [P, NTOK])
        root = m.sb("root", [P, NTOK])
        rstd = m.sb("rstd", [P, NTOK])
        corr = m.sb("corr", [P, NTOK])
        scale = m.sb("scale", [P, NTOK])
        ps = m.banks()

        const_in = m.sem("const_in")
        x_in = m.sems("x_in", XS)
        sumsq_done = m.sem("sumsq_done")
        mean_done = m.sem("mean_done")
        root_done = m.sem("root_done")
        x_scaled = m.sem("x_scaled")
        dve_step = m.sem("dve_step")
        x_turned = m.sem("x_turned")
        head_done = m.sem("head_done")
        tail_done = m.sem("tail_done")
        w_in_raw = m.sems("w_in_raw", RAW)
        w_head = m.sem("w_head")
        w_tail = m.sem("w_tail")
        mm_done = m.sem("mm_done")
        bias_ready = m.sem("bias_ready")
        evac_done = m.sem("evac_done")
        stored = m.sems("stored", STAGES)

        UQVK = 16
        NG = 16
        src_tile = [0, 1, 2, 3, 4, 5, 6, 7, 12, 13, 14, 15, 8, 9, 10, 11]
        slot = [0, 1, 2, 3, 4, 5, 4, 5, 0, 1, 2, 3, 4, 5, 4, 5]
        free_at = [0, 0, 0, 0, 0, 0, 20, 24, 16, 16, 16, 16, 28, 32, 52, 56]
        ng_evac = 16 + 16 + 16 + 16

        def bank(n):
            return 4 + n % 4 if n < NTOK else n % BANKS

        block = ctx.enter_context(nc.Block())

        @block.sync
        def _(sp):
            def load_w(t):
                if t >= RAW:
                    sp.wait_ge(w_tail, t - RAW + 1)
                sp.dma_start(wraw[:, t % RAW], w_in[src_tile[t]]).then_inc(w_in_raw[t % RAW], 16)

            def store(n, dst):
                sp.wait_ge(evac_done, n + 1)
                sp.dma_start(dst, stage[:, n % STAGES]).then_inc(stored[n % STAGES], 16)

            def load_x(t):
                if t >= XS:
                    sp.wait_ge(x_turned, t - XS + 1)
                sp.dma_start(xt[:, t % XS], x[t * P:(t + 1) * P, :]).then_inc(x_in[t % XS], 16)

            load_x(0)
            every = bass.AP(norm_g.tensor, norm_g.offset, [[0, P], [1, D]])
            for dst, src in ((ident, eye), (gain, every), (gbias, b_gate)):
                sp.dma_start(dst[:, :], src).then_inc(const_in, 16)
            load_w(0)
            load_w(1)
            load_x(1)
            load_w(2)
            load_w(3)
            for t in range(2, NTOK):
                load_x(t)
                if t < 4:
                    load_w(t + 2)
                if t > TPB:
                    n = t - TPB - 1
                    store(n, u_out[n * P:(n + 1) * P, :])
            for n in range(NTOK - TPB - 1, NTOK):
                store(n, u_out[n * P:(n + 1) * P, :])
            for t in range(6, 8):
                load_w(t)
            n = NTOK
            for q in range(4):
                load_w(8 + q)
                for b in range(NBLK):
                    store(n, qT_out[q * P:(q + 1) * P, b * BLK:(b + 1) * BLK])
                    n += 1
            for i in range(NTOK):
                if i % 4 == 0:
                    load_w(12 + i // 4)
                store(n, v_out[i * P:(i + 1) * P, :])
                n += 1

            def load_gate(t):
                sp.dma_start(wraw[:, t % RAW], w_in[16 + t]).then_inc(w_in_raw[t % RAW], 16)

            for q in range(4):
                if q >= 2:
                    sp.wait_ge(w_tail, UQVK + q - 2 - 1)
                    load_gate(q - 2)
                for b in range(NBLK):
                    store(n, kT_out[q * P:(q + 1) * P, b * BLK:(b + 1) * BLK])
                    n += 1
            with sp.Fori(0, NG // 2 - 1) as i:
                for j in range(2):
                    sp.wait_ge(w_tail, i * 2 + (UQVK + j + 1))
                    sp.dma_start(wraw[:, j], w_in[bass.ds(i * 2 + (18 + j), 1)].rearrange("o p k c -> (o p) k c")
                                 ).then_inc(w_in_raw[j], 16)
                    for b in range(NBLK):
                        sp.wait_ge(evac_done, i * 8 + (ng_evac + 4 * j + b + 1))
                        sp.dma_start(gT_out[bass.ds((i * 2 + j) * P, P), b * BLK:(b + 1) * BLK],
                                     stage[:, b]).then_inc(stored[b], 16)
            n = ng_evac + 4 * (NG - 2)
            for t in range(NG - 2, NG):
                for b in range(NBLK):
                    store(n, gT_out[t * P:(t + 1) * P, b * BLK:(b + 1) * BLK])
                    n += 1
            for s in range(STAGES):
                sp.wait_ge(stored[s], 16 * (n // STAGES))

        @block.gpsimd
        def _(pool):
            def tail(t, s):
                nc.gpsimd.tensor_tensor(w[:, 1, s], wraw[:, t % RAW], f32(w[:, 0, s]),
                                        ALU.subtract).then_inc(w_tail, 1)

            for t in range(UQVK):
                pool.wait_ge(w_head, t + 1)
                tail(t, slot[t])
            with pool.Fori(0, NG // 2) as i:
                for j in range(2):
                    pool.wait_ge(w_head, i * 2 + (UQVK + j + 1))
                    tail(j, 4 + j)

        @block.vector
        def _(dve):
            steps = [0]

            def after(ins):
                steps[0] += 1
                ins.then_inc(dve_step, 1)
                dve.wait_ge(dve_step, steps[0])

            def head(t):
                dve.wait_ge(w_in_raw[t % RAW], 16 * (t // RAW + 1))
                if free_at[t]:
                    dve.wait_ge(mm_done, free_at[t])
                nc.vector.tensor_copy(w[:, 0, slot[t]], wraw[:, t % RAW]).then_inc(w_head, 1)

            dve.wait_ge(const_in, 48)
            def mean_square(t):
                c = slice(t, t + 1)
                dve.wait_ge(sumsq_done, t + 1)
                nc.vector.tensor_scalar(mean[:, c], sumsq[:, c], 1.0 / D, EPS, ALU.mult, ALU.add).then_inc(mean_done, 1)

            def normalise(t):
                c = slice(t, t + 1)
                dve.wait_ge(root_done, t + 1)
                after(nc.vector.reciprocal(rstd[:, c], root[:, c]))
                after(nc.vector.tensor_scalar(corr[:, c], rstd[:, c], rstd[:, c], mean[:, c], ALU.mult, ALU.mult))
                after(nc.vector.tensor_scalar(scale[:, c], corr[:, c], -0.5, 1.5, ALU.mult, ALU.add))
                after(nc.vector.tensor_tensor(rstd[:, c], rstd[:, c], scale[:, c], ALU.mult))
                nc.vector.scalar_tensor_tensor(out=xt[:, t % XS], in0=xt[:, t % XS], scalar=rstd[:, c],
                                               in1=gain[:, :], op0=ALU.mult, op1=ALU.mult).then_inc(x_scaled, 1)

            def h_tails(t):
                for g in range(2):
                    dve.wait_ge(head_done, 2 * t + g + 1)
                    ks, at = slice(4 * g, 4 * g + 4), slice(t * P, (t + 1) * P)
                    nc.vector.tensor_tensor(hT[:, 1, ks, at], ps[:, 2 * (t % 2) + g].rearrange("p (k q) -> p k q", q=P),
                                            f32(hT[:, 0, ks, at]), ALU.subtract).then_inc(tail_done, 1)

            mean_square(0)
            normalise(0)
            head(0)
            head(1)
            mean_square(1)
            normalise(1)
            head(2)
            head(3)
            mean_square(2)
            h_tails(0)
            for t in range(NTOK):
                if t + 1 < NTOK:
                    h_tails(t + 1)
                if t + 2 < NTOK:
                    normalise(t + 2)
                if t + 3 < NTOK:
                    mean_square(t + 3)
                if t < 2:
                    head(4 + t)
            for t in range(6, UQVK):
                head(t)
            with dve.Fori(0, NG // 2) as i:
                for j in range(2):
                    dve.wait_ge(evac_done, i * 8 + (60 + 4 * j))
                    nc.vector.tensor_copy(bias_now[:, j:j + 1], gbias[:, bass.ds(i * 2 + j, 1)]).then_inc(bias_ready, 1)
                    dve.wait_ge(w_in_raw[j], i * 16 + 16 * (UQVK // 2 + 1))
                    dve.wait_ge(mm_done, i * 8 + (60 + 4 * j))
                    nc.vector.tensor_copy(w[:, 0, 4 + j], wraw[:, j]).then_inc(w_head, 1)

        @block.scalar
        def _(act):
            act.wait_ge(const_in, 48)

            def evac(n, func, **kw):
                act.wait_ge(mm_done, n + 1)
                if n >= STAGES:
                    act.wait_ge(stored[n % STAGES], 16 * (n // STAGES))
                nc.scalar.activation(stage[:, n % STAGES], ps[:, bank(n)], func, **kw).then_inc(evac_done, 1)

            def stats(t):
                act.wait_ge(x_in[t % XS], 16 * (t // XS + 1))
                if t:
                    act.wait_ge(sumsq_done, t)
                nc.scalar.activation(square[:, :], xt[:, t % XS], ACT.Square,
                                     accum_out=sumsq[:, t:t + 1]).then_inc(sumsq_done, 1)
                act.wait_ge(mean_done, t + 1)
                nc.scalar.activation(root[:, t:t + 1], mean[:, t:t + 1], ACT.Sqrt).then_inc(root_done, 1)

            def h_heads(t):
                act.wait_ge(x_turned, t + 1)
                for g in range(2):
                    nc.scalar.activation(hT[:, 0, 4 * g:4 * g + 4, t * P:(t + 1) * P],
                                         ps[:, 2 * (t % 2) + g].rearrange("p (k q) -> p k q", q=P),
                                         ACT.Copy).then_inc(head_done, 1)

            for t in range(3):
                stats(t)
            h_heads(0)
            for t in range(NTOK):
                if t:
                    evac(t - 1, ACT.Copy)
                if t + 1 < NTOK:
                    h_heads(t + 1)
                if t + 3 < NTOK:
                    stats(t + 3)
            evac(NTOK - 1, ACT.Copy)
            n = NTOK
            for _ in range(16):
                act.wait_ge(mm_done, n + 1)
                act.wait_ge(stored[n % STAGES], 16 * (n // STAGES))
                nc.scalar.activation(stage[:, n % STAGES].rearrange("p (j b c) -> p j b c", b=QR, c=QC),
                                     ps[:, n % BANKS].rearrange("p (b j c) -> p j b c", b=QR, c=QC)[:, :, ::-1],
                                     ACT.Copy, scale=HEAD_DIM ** -0.5).then_inc(evac_done, 1)
                n += 1
            for _ in range(32):
                evac(n, ACT.Copy)
                n += 1
            with act.Fori(0, NG // 2) as i:
                for j in range(2):
                    act.wait_ge(bias_ready, i * 2 + (j + 1))
                    for b in range(NBLK):
                        act.wait_ge(mm_done, i * 8 + (ng_evac + 4 * j + b + 1))
                        act.wait_ge(stored[b], i * 32 + 16 * (ng_evac // 4 + j))
                        nc.scalar.activation(stage[:, b], ps[:, 4 * j + b], ACT.Sigmoid,
                                             bias=bias_now[:, j:j + 1]).then_inc(evac_done, 1)

        @block.tensor
        def _(pe):
            pe.wait_ge(const_in, 48)

            def slab(n, t):
                before = n - 4 if n < NTOK else n - BANKS
                if before >= 0:
                    pe.wait_ge(evac_done, before + 1)
                for k in range(KD):
                    for a, b in SPLIT:
                        last = nc.tensor.matmul(ps[:, bank(n)], hT[:, a, k, t * P:(t + 1) * P], w[:, b, 0:4, k],
                                                start=(k == 0 and (a, b) == SPLIT[0]),
                                                stop=(k == KD - 1 and (a, b) == SPLIT[-1]))
                return last.then_inc(mm_done, 1)

            def tile(bank, s, b, first_wait):
                pe.wait_ge(evac_done, first_wait)
                for k in range(KD):
                    for a, c in SPLIT:
                        last = nc.tensor.matmul(ps[:, bank], w[:, a, s, k], hT[:, c, k, b * BLK:(b + 1) * BLK],
                                                start=(k == 0 and (a, c) == SPLIT[0]),
                                                stop=(k == KD - 1 and (a, c) == SPLIT[-1]))
                return last.then_inc(mm_done, 1)

            def turn(t):
                pe.wait_ge(x_scaled, t + 1)
                if t >= 2:
                    pe.wait_ge(tail_done, 2 * (t - 1))
                for k in range(KD):
                    last = nc.tensor.transpose(ps[:, 2 * (t % 2) + k // 4, (k % 4) * P:(k % 4 + 1) * P],
                                               xt[:, t % XS, k * P:(k + 1) * P], ident[:, :])
                last.then_inc(x_turned, 1)

            turn(0)
            for t in range(NTOK):
                if t + 1 < NTOK:
                    turn(t + 1)
                pe.wait_ge(tail_done, 2 * (t + 1))
                if t == 0:
                    pe.wait_ge(w_tail, 4)
                slab(t, t)
            n = NTOK

            def narrow(t, s, n):
                pe.wait_ge(w_tail, t + 1)
                for b in range(NBLK):
                    tile((n + b) % BANKS, s, b, n + b - BANKS + 1)

            for q in range(4):
                narrow(4 + q, slot[4 + q], n + 4 * q)
            n += 16
            pe.wait_ge(w_tail, 12)
            for t in range(NTOK):
                slab(n + t, t)
            n += NTOK
            for q in range(4):
                narrow(12 + q, slot[12 + q], n + 4 * q)
            with pe.Fori(0, NG // 2) as i:
                for j in range(2):
                    pe.wait_ge(w_tail, i * 2 + (UQVK + j + 1))
                    for b in range(NBLK):
                        tile(4 * j + b, 4 + j, b, i * 8 + (ng_evac + 4 * j + b - BANKS + 1))


ROWS = SEQ // GRID_W
KR, KC = 16, 32
TI, TJ = ROWS // QR, GRID_W // QC
ROW0 = [min(max(QR * i - ROW_WIN // 2, 0), ROWS - KR) for i in range(TI)]
COL0 = [min(max(QC * j - COL_WIN // 2, 0), GRID_W - KC) for j in range(TJ)]
KIND = [0, 1, 1, 2]
KINDS = 3
REL_R, REL_C = 31, 64
PAD_R, PAD_C = 8, 16
BASE_R = [ROW0[i] - QR * i + ROW_WIN - 1 + PAD_R for i in (0, 1, 3)]
BASE_C = [COL0[j] - QC * j + COL_WIN - 1 + PAD_C for j in (0, 1, 3)]
RPB_R, RPB_C = 2 * ROW_WIN - 1, 2 * COL_WIN - 1
NEG = -1.0e30


def fourier_phase(nc, u, pos_table, chan_table, fnT_out, rpb, padded, shifted):
    A = SEQ // P
    CW = 256
    CHUNKS = FNET_W // CW
    GPC = CW // P
    ND = A // 2 + 1
    XB = (ND + 1) // 2
    ORTHO = 1.0 / float(np.sqrt(SEQ * FNET_DIM))
    c1, c2, c3 = (float(np.cos(np.pi * i / 8)) for i in (1, 2, 3))
    USES = XB + 6
    with ExitStack() as ctx:
        m = Pool(nc, ctx, "ft")
        ub = m.sb("u", [P, CHUNKS, A, CW])
        st = m.sb("st", [P, A, CW])
        s4 = m.sb("s4", [P, 8, CW])
        s2 = m.sb("s2", [P, 4, CW])
        ab = m.sb("ab", [P, 2, CW])
        mn = m.sb("mn", [P, 6, CW])
        tmp = m.sb("tmp", [P, 8, CW])
        Y = m.sb("Y", [P, 2, A, CW], F32R)
        traw = m.sb("traw", [P, A, 2 * P])
        tab = m.sb("tab", [P, 2, A, 2 * P], F32R)
        craw = m.sb("craw", [P, 2, P])
        ctab = m.sb("ctab", [P, 2, 2, P], F32R)
        X = m.sb("X", [P, 2, 2 * XB, 2, P], F32R)
        real = m.sb("real", [P, 2, BLK])
        out = m.sb("out", [P, 1, SEQ])
        zero = m.sb("zero", [REL_R * 4, P])
        ps = m.banks()

        zeroed, filled, placed, shifted_done = (m.sem(x) for x in ("zeroed", "filled", "placed", "shifted_done"))
        tab_in, u_in = m.sem("tab_in"), m.sems("u_in", CHUNKS)
        tab_head, tab_tail = m.sem("tab_head"), m.sem("tab_tail")
        step = m.sem("step")
        y_ready, y_head, y_tail = m.sem("y_ready"), m.sem("y_head"), m.sem("y_tail")
        x_mm, x_head, x_tail = m.sem("x_mm"), m.sem("x_head"), m.sem("x_tail")
        out_mm, real_done, mirror_done = m.sem("out_mm"), m.sem("real_done"), m.sem("mirror_done")
        freed = m.sem("freed")
        stored = m.sem("stored")
        DS = [(0, 4), (4, 4), (8, 1)]

        block = ctx.enter_context(nc.Block())

        @block.sync
        def _(sp):
            u_v = u.rearrange("(a b) c -> b a c", b=P)
            sp.dma_start(ub[:, 0], u_v[:, :, 0:CW]).then_inc(u_in[0], 16)
            sp.dma_start(craw[:, :], chan_table).then_inc(tab_in, 16)
            sp.dma_start(traw[:, :], pos_table).then_inc(tab_in, 16)
            sp.dma_start(ub[:, 1], u_v[:, :, CW:2 * CW]).then_inc(u_in[1], 16)
            sp.wait_ge(zeroed, 1)
            sp.dma_start(padded.rearrange("h r (x c) -> (h r x) c", x=1).rearrange("(p y) c -> p (y c)", y=2),
                         zero[:, :]).then_inc(filled, 16)
            sp.wait_ge(filled, 16)
            sp.dma_start(padded[:, PAD_R:PAD_R + RPB_R, PAD_C:PAD_C + RPB_C], rpb).then_inc(placed, 16)
            sp.wait_ge(placed, 16)
            for j in range(KINDS):
                for c in range(QC):
                    sp.dma_start(shifted[j, :, c], padded[:, :, BASE_C[j] - c:BASE_C[j] - c + KC]
                                 ).then_inc(shifted_done, 16)
            for g in range(FNET_GROUPS):
                sp.wait_ge(mirror_done, 3 * (g + 1))
                sp.dma_start(fnT_out[g * P:(g + 1) * P, :], out[:, 0]).then_inc(stored, 16)
            sp.wait_ge(stored, 16 * FNET_GROUPS)
            sp.wait_ge(shifted_done, 16 * KINDS * QC)

        @block.gpsimd
        def _(pool):
            pool.wait_ge(tab_head, 1)
            nc.gpsimd.tensor_tensor(ctab[:, 1], craw[:, :], f32(ctab[:, 0]), ALU.subtract).then_inc(tab_tail, 1)
            pool.wait_ge(tab_head, 2)
            nc.gpsimd.tensor_tensor(tab[:, 1], traw[:, :], f32(tab[:, 0]), ALU.subtract).then_inc(tab_tail, 1)
            for h in range(CHUNKS):
                for e in range(2):
                    pool.wait_ge(y_head, 2 * h + e + 1)
                    nc.gpsimd.tensor_tensor(Y[:, 1, e::2], ub[:, h, e::2], f32(Y[:, 0, e::2]),
                                            ALU.subtract).then_inc(y_tail, 1)

        @block.vector
        def _(dve):
            V = nc.vector
            done = [0]

            def op(ins):
                done[0] += 1
                ins.then_inc(step, 1)
                return done[0]

            def after(n):
                dve.wait_ge(step, n)

            def mac(o, a, k, b, op1=ALU.add):
                return op(V.scalar_tensor_tensor(out=o, in0=a, scalar=k, in1=b, op0=ALU.mult, op1=op1))

            def tt(o, a, b, f):
                return op(V.tensor_tensor(o, a, b, f))

            def dft16(h):
                y = ub[:, h]
                dve.wait_ge(u_in[h], 16)
                if done[0]:
                    after(done[0])
                tt(st[:, 0:8], y[:, 0:8], y[:, 8:16], ALU.add)
                n = tt(st[:, 8:16], y[:, 0:8], y[:, 8:16], ALU.subtract)
                t = st[:, 8:16]
                after(n)
                tt(s4[:, 0:4], st[:, 0:4], st[:, 4:8], ALU.add)
                tt(s4[:, 4:8], st[:, 0:4], st[:, 4:8], ALU.subtract)
                tt(mn[:, 0:3], t[:, 1:4], t[:, 7:4:-1], ALU.subtract)
                n = tt(mn[:, 3:6], t[:, 1:4], t[:, 7:4:-1], ALU.add)
                after(n)
                tt(s2[:, 0:2], s4[:, 0:2], s4[:, 2:4], ALU.add)
                tt(y[:, 4:13:8], s4[:, 0:2], s4[:, 2:4], ALU.subtract)
                tt(ab[:, 0], s4[:, 5], s4[:, 7], ALU.subtract)
                n = tt(ab[:, 1], s4[:, 5], s4[:, 7], ALU.add)
                after(n)
                tt(y[:, 0], s2[:, 0], s2[:, 1], ALU.add)
                tt(y[:, 8], s2[:, 0], s2[:, 1], ALU.subtract)
                mac(y[:, 2], ab[:, 0], c2, s4[:, 4])
                mac(y[:, 6], ab[:, 0], -c2, s4[:, 4])
                mac(y[:, 10], ab[:, 1], c2, s4[:, 6])
                n = mac(y[:, 14], ab[:, 1], -c2, s4[:, 6])
                after(n)
                V.engine_nop().then_inc(y_ready, 1)
                mac(tmp[:, 0], mn[:, 1], c2, t[:, 0])
                mac(tmp[:, 1], mn[:, 1], -c2, t[:, 0])
                mac(tmp[:, 2], mn[:, 2], c3 / c1, mn[:, 0])
                mac(tmp[:, 3], mn[:, 2], -c1 / c3, mn[:, 0])
                mac(tmp[:, 4], mn[:, 4], c2, t[:, 4])
                mac(tmp[:, 5], mn[:, 4], c2, t[:, 4], ALU.subtract)
                mac(tmp[:, 6], mn[:, 5], -c3 / c1, mn[:, 3])
                n = mac(tmp[:, 7], mn[:, 3], c3 / c1, mn[:, 5])
                after(n)
                mac(y[:, 1], tmp[:, 2], c1, tmp[:, 0])
                mac(y[:, 7], tmp[:, 2], -c1, tmp[:, 0])
                mac(y[:, 3], tmp[:, 3], c3, tmp[:, 1])
                mac(y[:, 5], tmp[:, 3], -c3, tmp[:, 1])
                mac(y[:, 9], tmp[:, 7], c1, tmp[:, 4])
                mac(y[:, 15], tmp[:, 7], c1, tmp[:, 4], ALU.subtract)
                mac(y[:, 11], tmp[:, 6], c1, tmp[:, 5])
                n = mac(y[:, 13], tmp[:, 6], c1, tmp[:, 5], ALU.subtract)
                after(n)
                V.engine_nop().then_inc(y_ready, 1)

            def group(g):
                for j in range(XB):
                    w = 2 * P * min(2, ND - 2 * j)
                    dve.wait_ge(x_head, XB * g + j + 1)
                    V.tensor_tensor(X[:, 1, 2 * j:2 * j + 2].rearrange("p d r c -> p (d r c)")[:, 0:w],
                                    ps[:, (USES * g + j) % BANKS, 0:w],
                                    f32(X[:, 0, 2 * j:2 * j + 2]).rearrange("p d r c -> p (d r c)")[:, 0:w],
                                    ALU.subtract).then_inc(x_tail, 1)
                o = out[:, 0].rearrange("p (c d) -> p d c", d=A)
                if g:
                    dve.wait_ge(stored, 16 * g)
                for q, (d, w) in enumerate(DS):
                    imag = ps[:, (USES * g + XB + 2 * q + 1) % BANKS, 0:w * P].rearrange("p (d c) -> p d c", c=P)
                    re = real[:, (3 * g + q) % 2, 0:w * P].rearrange("p (d c) -> p d c", c=P)
                    dve.wait_ge(real_done, 3 * g + q + 1)
                    ins = V.scalar_tensor_tensor(out=o[:, d:d + w], in0=imag, scalar=ORTHO, in1=re,
                                                 op0=ALU.mult, op1=ALU.add)
                    f = max(d, 1)
                    if d + w <= ND - 1:
                        a, b = A - f, A - (d + w)
                        ins = V.scalar_tensor_tensor(out=o[:, a:b:-1, ::-1], in0=imag[:, f - d:], scalar=-ORTHO,
                                                     in1=re[:, f - d:], op0=ALU.mult, op1=ALU.add)
                    ins.then_inc(mirror_done, 1)

            V.memset(zero[:, :], 0.0).then_inc(zeroed, 1)
            dft16(0)
            dft16(1)
            for g in range(FNET_GROUPS):
                group(g)

        @block.scalar
        def _(act):
            act.wait_ge(tab_in, 32)
            nc.scalar.activation(ctab[:, 0], craw[:, :], ACT.Copy).then_inc(tab_head, 1)
            nc.scalar.activation(tab[:, 0], traw[:, :], ACT.Copy).then_inc(tab_head, 1)

            def heads(h):
                for e in range(2):
                    act.wait_ge(y_ready, 2 * h + e + 1)
                    if h:
                        act.wait_ge(x_mm, XB * GPC * h)
                    nc.scalar.activation(Y[:, 0, e::2], ub[:, h, e::2], ACT.Copy).then_inc(y_head, 1)

            def group(g):
                for j in range(XB):
                    w = 2 * P * min(2, ND - 2 * j)
                    act.wait_ge(x_mm, XB * g + j + 1)
                    if g:
                        act.wait_ge(out_mm, 3 * g)
                    nc.scalar.activation(X[:, 0, 2 * j:2 * j + 2].rearrange("p d r c -> p (d r c)")[:, 0:w],
                                         ps[:, (USES * g + j) % BANKS, 0:w], ACT.Copy).then_inc(x_head, 1)
                for q, (d, w) in enumerate(DS):
                    n = 3 * g + q
                    act.wait_ge(out_mm, n + 1)
                    if n >= 2:
                        act.wait_ge(mirror_done, n - 1)
                    nc.scalar.activation(real[:, n % 2, 0:w * P], ps[:, (USES * g + XB + 2 * q) % BANKS, 0:w * P],
                                         ACT.Copy, scale=ORTHO).then_inc(real_done, 1)

            heads(0)
            for g in range(FNET_GROUPS):
                if g == 1:
                    heads(1)
                group(g)

        @block.tensor
        def _(pe):
            def claim(n):
                if n < BANKS:
                    return
                g, j = divmod(n - BANKS, USES)
                if j < XB:
                    pe.wait_ge(x_tail, XB * g + j + 1)
                else:
                    pe.wait_ge(mirror_done, 3 * g + (j - XB) // 2 + 1)

            for g in range(FNET_GROUPS):
                h, c0 = g // GPC, (g % GPC) * P
                pe.wait_ge(tab_tail, 2)
                pe.wait_ge(y_tail, 2 * h + 2)
                for j in range(XB):
                    n = USES * g + j
                    claim(n)
                    for d in range(2 * j, min(2 * j + 2, ND)):
                        parts = [d] if d in (0, 8) else [d, 8 + d]
                        mms = [(i, a, b) for i in parts for a, b in SPLIT]
                        for q, (i, a, b) in enumerate(mms):
                            last = nc.tensor.matmul(ps[:, n % BANKS, (d % 2) * 256:(d % 2) * 256 + 256],
                                                    Y[:, a, i, c0:c0 + P], tab[:, b, i],
                                                    start=(q == 0), stop=(q == len(mms) - 1))
                    last.then_inc(x_mm, 1)
                pe.wait_ge(x_tail, XB * (g + 1))
                for q, (d, w) in enumerate(DS):
                    for r in range(2):
                        n = USES * g + XB + 2 * q + r
                        claim(n)
                        for i, (a, b) in enumerate(SPLIT):
                            last = nc.tensor.matmul(ps[:, n % BANKS, 0:w * P], ctab[:, a, r], X[:, b, d:d + w, r],
                                                    start=(i == 0), stop=(i == 2))
                    last.then_inc(out_mm, 1)


def fourier_tables():
    A, N = SEQ // P, SEQ
    b, c = np.arange(P)[:, None], np.arange(P)[None, :]
    pos = np.zeros((P, A, 2 * P), np.float64)
    for d in range(A // 2 + 1):
        th = 2 * np.pi * ((b * (A * c + d)) % N) / N
        pos[:, d] = np.concatenate([np.cos(th), -np.sin(th)], 1)
        if 0 < d < 8:
            sign = 1.0 if d == 6 else -1.0
            pos[:, 8 + d] = sign * np.concatenate([np.sin(th), np.cos(th)], 1)
    th = 2 * np.pi * ((b * c) % FNET_DIM) / FNET_DIM
    chan = np.stack([np.cos(th), np.sin(th)], 1)
    return pos.astype(np.float32), chan.astype(np.float32)


def window_mask():
    out = np.full((KINDS * KINDS, QR, QC, KR, KC), NEG, np.float32)
    for a, i in enumerate((0, 1, 3)):
        for b, j in enumerate((0, 1, 3)):
            r = QR * i + np.arange(QR)[::-1]
            c = QC * j + np.arange(QC)
            r0 = np.clip(r - ROW_WIN // 2, 0, ROWS - ROW_WIN)[:, None]
            c0 = np.clip(c - COL_WIN // 2, 0, GRID_W - COL_WIN)[:, None]
            kr = ROW0[i] + np.arange(KR)[None, :]
            kc = COL0[j] + np.arange(KC)[None, :]
            rin = (kr >= r0) & (kr < r0 + ROW_WIN)
            cin = (kc >= c0) & (kc < c0 + COL_WIN)
            out[a * KINDS + b][rin[:, None, :, None] & cin[None, :, None, :]] = 0.0
    return out.reshape(KINDS * KINDS, P, KR * KC).transpose(1, 0, 2).copy()


def attention_phase(nc, qT, kT, v, shifted, mask, eye, atT_out):
    KT = KR * KC // P
    VG = ROWS // 4
    TILES = TI * TJ
    N = HEADS * TILES
    NB = KINDS * KINDS
    PARTS = 4
    SB, PTB, OB, TB = (0, 1, 2), (3, 4), (5, 6), 7
    with ExitStack() as ctx:
        m = Pool(nc, ctx, "at")
        qraw = m.sb("qraw", [P, ROWS, GRID_W])
        kraw = m.sb("kraw", [P, ROWS, GRID_W])
        vs = m.sb("vs", [P, 2, VG * TJ, HEAD_DIM])
        qs = m.sb("qs", [P, 2, ROWS, GRID_W], F32R)
        kh = m.sb("kh", [P, 2, ROWS, GRID_W], F32R)
        kl = m.sb("kl", [P, 2, ROWS, GRID_W], F32R)
        bias = m.sb("bias", [P, 2, NB, KR * KC])
        window = m.sb("window", [P, NB, KR * KC])
        neg = m.sb("neg", [P, 3, KR * KC])
        prob = m.sb("prob", [P, 3, KR * KC])
        pT = m.sb("pT", [P, 3, KT, P])
        o = m.sb("o", [P, 2, TILES, 2 * HEAD_DIM])
        atT = m.sb("atT", [P, ROWS, GRID_W])
        ident = m.sb("ident", [P, P])
        negmax = m.sb("negmax", [P, N])
        total = m.sb("total", [P, N])
        inverse = m.sb("inverse", [P, N])
        ps = m.banks()

        const_in = m.sem("const_in")
        qk_in, v_in, bias_in = m.sem("qk_in"), m.sems("v_in", 2), m.sems("bias_in", 2)
        qk_heads, q_tail, k_tail, bias_ready = (m.sem(x) for x in ("qk_heads", "q_tail", "k_tail", "bias_ready"))
        s_mm, s_red, p_exp, pT_mm, pT_copied, o_mm, inverted, o_done = (
            m.sem(x) for x in ("s_mm", "s_red", "p_exp", "pT_mm", "pT_copied", "o_mm", "inverted", "o_done"))
        turned, evac, stored = m.sem("turned"), m.sem("evac"), m.sem("stored")

        def where(n):
            h, t = divmod(n, TILES)
            return h, t, t // TJ, t % TJ

        def turn_at(n):
            pair, t = divmod(n, 2 * TILES)
            if pair and t in (3, 5, 7, 9):
                return pair - 1, (t - 3) // 2
            return None

        block = ctx.enter_context(nc.Block())

        @block.sync
        def _(sp):
            sp.dma_start(ident[:, :], eye).then_inc(const_in, 16)

            def load(h):
                if h:
                    sp.wait_ge(q_tail, h)
                    sp.wait_ge(k_tail, h)
                for half in range(2):
                    for dst, src in ((qraw, qT), (kraw, kT)):
                        sp.dma_start(dst[half * HEAD_DIM:(half + 1) * HEAD_DIM].rearrange("p r c -> p (r c)"),
                                     src[h * HEAD_DIM:(h + 1) * HEAD_DIM, :]).then_inc(qk_in, 16)
                if h >= 2:
                    sp.wait_ge(s_red, TILES * (h - 1))
                for i in range(KINDS):
                    for j in range(KINDS):
                        rows = shifted[j, h]
                        src = bass.AP(rows.tensor, rows.offset + (BASE_R[i] - (QR - 1)) * KC,
                                      [[KC, QR], [REL_R * KC, QC], [1, KR * KC]])
                        sp.dma_start(bias[:, h % 2, i * KINDS + j], src).then_inc(bias_in[h % 2], 16)
                if h == 0:
                    sp.dma_start(window[:, :], mask).then_inc(const_in, 16)
                if h >= 2:
                    sp.wait_ge(o_mm, TILES * (h - 1))
                vv = v.rearrange("(g r c) f -> r c g f", r=4, c=GRID_W)
                for r in range(4):
                    for j in range(TJ):
                        sp.dma_start(vs[r * KC:(r + 1) * KC, h % 2, j::TJ],
                                     vv[r, COL0[j]:COL0[j] + KC, :, h * HEAD_DIM:(h + 1) * HEAD_DIM]
                                     ).then_inc(v_in[h % 2], 16)

            def store(pair):
                sp.wait_ge(evac, 4 * (pair + 1))
                sp.dma_start(atT_out[pair * P:(pair + 1) * P, :], atT[:, :]).then_inc(stored, 16)

            for h in range(HEADS):
                load(h)
                if h >= 4 and h % 2 == 0:
                    store((h - 4) // 2)
            for pair in range((HEADS - 3) // 2, HEADS // 2):
                store(pair)
            sp.wait_ge(stored, 16 * (HEADS // 2))

        @block.gpsimd
        def _(pool):
            G = nc.gpsimd
            for h in range(HEADS):
                s = h % 2
                pool.wait_ge(qk_heads, 2 * PARTS * h + PARTS)
                up = slice(HEAD_DIM, P)
                if h > 1:
                    pool.wait_ge(k_tail, h)
                G.tensor_tensor(qs[up, s], qraw[up], f32(qs[up, s]), ALU.subtract).then_inc(q_tail, 1)
                if h:
                    pool.wait_ge(qk_heads, 2 * PARTS * (h + 1))
                    pool.wait_ge(q_tail, h + 1)
                    G.tensor_tensor(kl[:, s], kraw[:, :], f32(kh[:, s]), ALU.subtract).then_inc(k_tail, 1)

        @block.vector
        def _(dve):
            V = nc.vector

            def reduce(n):
                h, t, i, j = where(n)
                dve.wait_ge(s_mm, n + 1)
                kind = KIND[i] * KINDS + KIND[j]
                dve.wait_ge(bias_ready, h * NB + kind + 1)
                if n >= 3:
                    dve.wait_ge(p_exp, n - 2)
                V.tensor_tensor_reduce(out=neg[:, n % 3], in0=ps[:, SB[n % 3]],
                                       in1=bias[:, h % 2, kind], scale=-1.0, scalar=3.0e38,
                                       op0=ALU.add, op1=ALU.min, accum_out=negmax[:, n:n + 1]).then_inc(s_red, 1)

            def copy(n):
                dve.wait_ge(pT_mm, n + 1)
                if n >= 3:
                    dve.wait_ge(o_mm, n - 2)
                V.tensor_copy(pT[:, n % 3], ps[:, PTB[n % 2]].rearrange("p (k q) -> p k q", k=KT)).then_inc(pT_copied, 1)

            def invert(n):
                dve.wait_ge(p_exp, n + 1)
                V.reciprocal(inverse[:, n:n + 1], total[:, n:n + 1]).then_inc(inverted, 1)

            def masked_bias(n):
                h, t, i, j = where(n)
                kind = KIND[i] * KINDS + KIND[j]
                if i == 2 or j == 2:
                    return
                dve.wait_ge(bias_in[h % 2], 16 * NB * (h // 2 + 1))
                b = bias[:, h % 2, kind]
                V.tensor_tensor(b, b, window[:, kind], ALU.add).then_inc(bias_ready, 1)

            dve.wait_ge(qk_heads, 2 * PARTS)
            V.tensor_tensor(kl[:, 0], kraw[:, :], f32(kh[:, 0]), ALU.subtract).then_inc(k_tail, 1)
            dve.wait_ge(const_in, 32)
            masked_bias(0)
            for n in range(-4, N):
                if 0 <= n + 3 < N:
                    reduce(n + 3)
                if 0 < n + 4 < N:
                    masked_bias(n + 4)
                if 0 <= n + 1 < N:
                    copy(n + 1)
                    invert(n + 1)

        @block.scalar
        def _(act):
            def qk_head(h, part):
                s = h % 2
                r = slice(part % PARTS * ROWS // PARTS, (part % PARTS + 1) * ROWS // PARTS)
                if part == 0:
                    act.wait_ge(qk_in, 64 * (h + 1))
                    if h >= 2:
                        act.wait_ge(s_mm, TILES * (h - 1))
                dst = (qs, kh)[part // PARTS]
                src = (qraw, kraw)[part // PARTS]
                nc.scalar.activation(dst[:, s, r], src[:, r], ACT.Copy).then_inc(qk_heads, 1)

            def exp(n):
                act.wait_ge(s_red, n + 1)
                if n >= 3:
                    act.wait_ge(pT_mm, n - 2)
                nc.scalar.activation(prob[:, n % 3], neg[:, n % 3], ACT.Exp, scale=-1.0, bias=negmax[:, n:n + 1],
                                     accum_out=total[:, n:n + 1]).then_inc(p_exp, 1)

            def divide(n):
                h, t, _, _ = where(n)
                act.wait_ge(o_mm, n + 1)
                act.wait_ge(inverted, n + 1)
                pair = h // 2
                if pair >= 2 and h % 2 == 0 and t == 0:
                    act.wait_ge(turned, 4 * (pair - 1))
                nc.scalar.activation(o[:, pair % 2, t, (h % 2) * HEAD_DIM:(h % 2 + 1) * HEAD_DIM],
                                     ps[:, OB[n % 2], 0:HEAD_DIM], ACT.Copy,
                                     scale=inverse[:, n:n + 1]).then_inc(o_done, 1)

            def turn(pair, i):
                act.wait_ge(turned, 4 * pair + i + 1)
                if pair and i == 0:
                    act.wait_ge(stored, 16 * pair)
                nc.scalar.activation(
                    atT[:, i * QR:(i + 1) * QR].rearrange("p b (j c) -> p j b c", c=QC),
                    ps[:, TB].rearrange("p (j b c) -> p j b c", b=QR, c=QC)[:, :, ::-1], ACT.Copy).then_inc(evac, 1)

            for part in range(2 * PARTS):
                qk_head(0, part)
            for n in range(-4, N + 1):
                h, t, _, _ = where(max(n, 0))
                if n >= 1:
                    divide(n - 1)
                if 0 <= n + 3 < N:
                    exp(n + 3)
                if 0 <= n < N:
                    if n and turn_at(n - 1):
                        turn(*turn_at(n - 1))
                    if h + 1 < HEADS and t < 2 * PARTS:
                        qk_head(h + 1, t)
            for i in range(TI):
                turn(HEADS // 2 - 1, i)

        @block.tensor
        def _(pe):
            def scores(n):
                h, t, i, j = where(n)
                if t == 0:
                    pe.wait_ge(q_tail, h + 1)
                    pe.wait_ge(k_tail, h + 1)
                if n >= 3:
                    pe.wait_ge(s_red, n - 2)
                q = qs[:, h % 2, 2 * t:2 * t + 2].rearrange("p r c -> p (r c)")
                for k in (kh, kl):
                    last = nc.tensor.matmul(ps[:, SB[n % 3]], q,
                                            k[:, h % 2, ROW0[i]:ROW0[i] + KR, COL0[j]:COL0[j] + KC],
                                            start=(k is kh), stop=(k is kl))
                last.then_inc(s_mm, 1)

            def transpose(n):
                pe.wait_ge(p_exp, n + 1)
                if n >= 2:
                    pe.wait_ge(pT_copied, n - 1)
                for k in range(KT):
                    last = nc.tensor.transpose(ps[:, PTB[n % 2], k * P:(k + 1) * P],
                                               prob[:, n % 3, k * P:(k + 1) * P], ident[:, :])
                last.then_inc(pT_mm, 1)

            def values(n):
                h, t, i, j = where(n)
                pe.wait_ge(pT_copied, n + 1)
                if t == 0:
                    pe.wait_ge(v_in[h % 2], 16 * 4 * TJ * (h // 2 + 1))
                if n >= 2:
                    pe.wait_ge(o_done, n - 1)
                for k in range(KT):
                    last = nc.tensor.matmul(ps[:, OB[n % 2], 0:HEAD_DIM], pT[:, n % 3, k],
                                            vs[:, h % 2, (ROW0[i] // 4 + k) * TJ + j],
                                            start=(k == 0), stop=(k == KT - 1))
                last.then_inc(o_mm, 1)

            def turn(pair, i):
                pe.wait_ge(o_done, 2 * TILES * (pair + 1))
                if pair or i:
                    pe.wait_ge(evac, 4 * pair + i)
                for j in range(TJ):
                    last = nc.tensor.transpose(ps[:, TB, j * P:(j + 1) * P], o[:, pair % 2, i * TJ + j], ident[:, :])
                last.then_inc(turned, 1)

            pe.wait_ge(const_in, 16)
            for n in range(-4, N):
                if n + 4 < N:
                    scores(n + 4)
                if 0 <= n + 2 < N:
                    transpose(n + 2)
                if n >= 0:
                    values(n)
                    if turn_at(n - 1):
                        turn(*turn_at(n - 1))
            for i in range(TI):
                turn(HEADS // 2 - 1, i)


def at_least(engine, sem, value):
    if value > 0:
        engine.wait_ge(sem, value)


def mixer_output_phase(nc, x, fnT, atT, gT, w_mix, w_out, norm_g, eye, x2_out, hT_out):
    KA = (FNET_W + NA_W) // P
    HALF = D // 2
    SPH = HALF // P
    with ExitStack() as ctx:
        m = Pool(nc, ctx, "mo")
        araw = m.sb("araw", [P, 4, BLK])
        act_s = m.sb("act", [P, 2, KA, BLK], F32R)
        mixed = m.sb("mixed", [P, 2, KD, BLK], F32R)
        w = m.sb("w", [P, 2, 2, KA, P], F32R)
        wo = m.sb("wo", [P, 2, KD, KD, P], F32R)
        wraw = m.sb("wraw", [P, 2, KD, P])
        gate = m.sb("gate", [P, 2, 2, BLK])
        prod = m.sb("prod", [P, 2, BLK])
        mix = m.sb("mix", [P, 2, BLK])
        xt = m.sb("xt", [P, 3, D])
        h2 = m.sb("h2", [P, 2, D])
        turned_sb = m.sb("turned", [P, 1, KD, P])
        square = m.sb("square", [P, D], BF16)
        ident = m.sb("ident", [P, P])
        gain = m.sb("gain", [P, KD])
        sumsq, mean, root, rstd, corr, scale = (
            m.sb(s, [P, NTOK]) for s in ("sumsq", "mean", "root", "rstd", "corr", "scale"))
        ps = m.banks()

        const_in, a_in, w_in_raw, g_in, x_in = (
            m.sem("const_in"), m.sems("a_in", 4), m.sems("w_in", 2), m.sems("g_in", 2), m.sems("x_in", 3))
        a_head, a_tail, w_head, w_tail = (m.sem(s) for s in ("a_head", "a_tail", "w_head", "w_tail"))
        branch_mm, step, multiplied, mix_done, mix_head, mix_tail = (
            m.sem(s) for s in ("branch_mm", "step", "multiplied", "mix_done", "mix_head", "mix_tail"))
        out_mm, x2_done, sumsq_done, mean_done, root_done, h2_done = (
            m.sem(s) for s in ("out_mm", "x2_done", "sumsq_done", "mean_done", "root_done", "h2_done"))
        turned, evac = m.sem("turned_mm"), m.sem("evac")
        x2_stored, hT_stored = m.sems("x2_stored", 3), m.sem("hT_stored")

        order = [("mix", 0)]
        for b in range(NBLK):
            for s in range(KD):
                if s < KD - 1 or b < NBLK - 1:
                    order.append(("mix", (s + 1) % KD))
                order.append(("out", s))
        def w_index(b, kind, s):
            if kind == "mix":
                return 16 * b + (2 * s - 1 if s else (0 if b == 0 else -2))
            last = b == NBLK - 1 and s == KD - 1
            return 16 * b + 2 * s + (1 if last else 2)

        block = ctx.enter_context(nc.Block())

        @block.sync
        def _(sp):
            sp.dma_start(ident[:, :], eye).then_inc(const_in, 16)
            sp.dma_start(gain[:, :], norm_g).then_inc(const_in, 16)
            count = [0]

            def load_w():
                n = count[0]
                count[0] += 1
                at_least(sp, w_tail, n - 1)
                kind, t = order[n]
                sp.dma_start(wraw[:, n % 2], (w_mix if kind == "mix" else w_out)[t]).then_inc(w_in_raw[n % 2], 16)

            def load_a(b, k):
                n = b * KA + k
                at_least(sp, a_tail, n - 3)
                src = fnT if k < KA // 2 else atT
                r = (k % (KA // 2)) * P
                sp.dma_start(araw[:, n % 4], src[r:r + P, b * BLK:(b + 1) * BLK]).then_inc(a_in[n % 4], 16)

            load_w()
            for k in range(KA):
                load_a(0, k)
            for b in range(NBLK):
                for s in range(KD):
                    n = b * KD + s
                    at_least(sp, mix_done, n - 1)
                    for branch in range(2):
                        r = branch * D + s * P
                        sp.dma_start(gate[:, n % 2, branch], gT[r:r + P, b * BLK:(b + 1) * BLK]
                                     ).then_inc(g_in[n % 2], 16)
                    if s < KD - 1 or b < NBLK - 1:
                        load_w()
                    load_w()
                for t in range(TPB):
                    n = b * TPB + t
                    at_least(sp, h2_done, n - 2)
                    if n >= 3:
                        sp.wait_ge(x2_stored[n % 3], 16 * (n // 3))
                    sp.dma_start(xt[:, n % 3], x[n * P:(n + 1) * P, :]).then_inc(x_in[n % 3], 16)
                    if b < NBLK - 1:
                        load_a(b + 1, 2 * t)
                        load_a(b + 1, 2 * t + 1)

        @block.gpsimd
        def _(pool):
            count = [0]

            def w_tails(number):
                for _ in range(number):
                    n = count[0]
                    count[0] += 1
                    kind, t = order[n]
                    pool.wait_ge(w_head, n + 1)
                    dst = w[:, :, t % 2] if kind == "mix" else wo[:, :, :, t]
                    nc.gpsimd.tensor_tensor(dst[:, 1], wraw[:, n % 2], f32(dst[:, 0]), ALU.subtract).then_inc(w_tail, 1)

            def a_tails(b, k):
                n = b * KA + k
                pool.wait_ge(a_head, n + 1)
                nc.gpsimd.tensor_tensor(act_s[:, 1, k], araw[:, n % 4], f32(act_s[:, 0, k]),
                                        ALU.subtract).then_inc(a_tail, 1)

            w_tails(1)
            for k in range(KA):
                a_tails(0, k)
            for b in range(NBLK):
                for s in range(KD):
                    w_tails(2 if s < KD - 1 or b < NBLK - 1 else 1)
                if b < NBLK - 1:
                    for k in range(KA):
                        a_tails(b + 1, k)

        @block.vector
        def _(dve):
            V = nc.vector
            count, steps = [0], [0]

            def after(ins):
                steps[0] += 1
                ins.then_inc(step, 1)
                dve.wait_ge(step, steps[0])

            def w_heads(b, s, number):
                for _ in range(number):
                    n = count[0]
                    count[0] += 1
                    kind, t = order[n]
                    dve.wait_ge(w_in_raw[n % 2], 16 * (n // 2 + 1))
                    if kind == "mix":
                        at_least(dve, branch_mm, 2 * (b * KD + s))
                        dst = w[:, 0, t % 2]
                    else:
                        at_least(dve, out_mm, 2 * TPB * b)
                        dst = wo[:, 0, :, t]
                    V.tensor_copy(dst, wraw[:, n % 2]).then_inc(w_head, 1)

            def a_heads(b, k):
                n = b * KA + k
                dve.wait_ge(a_in[n % 4], 16 * (n // 4 + 1))
                at_least(dve, branch_mm, 2 * KD * b)
                V.tensor_copy(act_s[:, 0, k], araw[:, n % 4]).then_inc(a_head, 1)

            def gated(b, s):
                n = b * KD + s
                dve.wait_ge(g_in[n % 2], 32 * (n // 2 + 1))
                at_least(dve, mix_done, n)
                for branch in range(2):
                    dve.wait_ge(branch_mm, 2 * n + branch + 1)
                    V.tensor_tensor(prod[:, branch], ps[:, 2 * (n % 2) + branch], gate[:, n % 2, branch],
                                    ALU.mult).then_inc(multiplied, 1)
                dve.wait_ge(multiplied, 2 * n + 2)
                at_least(dve, mix_tail, n - 1)
                V.tensor_tensor(mix[:, n % 2], prod[:, 0], prod[:, 1], ALU.add).then_inc(mix_done, 1)

            def mix_tails(n):
                dve.wait_ge(mix_head, n + 1)
                V.tensor_tensor(mixed[:, 1, n % KD], mix[:, n % 2], f32(mixed[:, 0, n % KD]),
                                ALU.subtract).then_inc(mix_tail, 1)

            def finish(b, t):
                n = b * TPB + t
                c = slice(n, n + 1)
                dve.wait_ge(x_in[n % 3], 16 * (n // 3 + 1))
                for half in range(2):
                    dve.wait_ge(out_mm, 2 * n + half + 1)
                    part = xt[:, n % 3, half * HALF:(half + 1) * HALF]
                    V.tensor_tensor(part, ps[:, 4 + half], part, ALU.add).then_inc(x2_done, 1)
                dve.wait_ge(sumsq_done, n + 1)
                V.tensor_scalar(mean[:, c], sumsq[:, c], 1.0 / D, EPS, ALU.mult, ALU.add).then_inc(mean_done, 1)
                dve.wait_ge(root_done, n + 1)
                after(V.reciprocal(rstd[:, c], root[:, c]))
                after(V.tensor_scalar(corr[:, c], rstd[:, c], rstd[:, c], mean[:, c], ALU.mult, ALU.mult))
                after(V.tensor_scalar(scale[:, c], corr[:, c], -0.5, 1.5, ALU.mult, ALU.add))
                after(V.tensor_tensor(rstd[:, c], rstd[:, c], scale[:, c], ALU.mult))
                at_least(dve, turned, n - 1)
                V.tensor_scalar(h2[:, n % 2], xt[:, n % 3], rstd[:, c], None, ALU.mult).then_inc(h2_done, 1)

            w_heads(0, 0, 1)
            for k in range(KA):
                a_heads(0, k)
            for b in range(NBLK):
                for s in range(KD):
                    w_heads(b, s, 2 if s < KD - 1 or b < NBLK - 1 else 1)
                    gated(b, s)
                    if s:
                        mix_tails(b * KD + s - 1)
                mix_tails(b * KD + KD - 1)
                for t in range(TPB):
                    finish(b, t)
                    if b < NBLK - 1:
                        a_heads(b + 1, 2 * t)
                        a_heads(b + 1, 2 * t + 1)

        @block.scalar
        def _(act):
            act.wait_ge(const_in, 32)

            def mix_heads(n):
                act.wait_ge(mix_done, n + 1)
                if n >= KD:
                    act.wait_ge(out_mm, 2 * TPB * (n // KD))
                nc.scalar.activation(mixed[:, 0, n % KD], mix[:, n % 2], ACT.Copy).then_inc(mix_head, 1)

            def stats(n):
                act.wait_ge(x2_done, 2 * n + 2)
                at_least(act, sumsq_done, n)
                nc.scalar.activation(square[:, :], xt[:, n % 3], ACT.Square,
                                     accum_out=sumsq[:, n:n + 1]).then_inc(sumsq_done, 1)
                act.dma_start(x2_out[n * P:(n + 1) * P, :], xt[:, n % 3]).then_inc(x2_stored[n % 3], 16)
                act.wait_ge(mean_done, n + 1)
                nc.scalar.activation(root[:, n:n + 1], mean[:, n:n + 1], ACT.Sqrt).then_inc(root_done, 1)

            def spill(n):
                act.wait_ge(turned, n + 1)
                if n:
                    act.wait_ge(hT_stored, 16 * n)
                for k in range(KD):
                    nc.scalar.activation(turned_sb[:, 0, k], ps[:, 6 + k // 4, (k % 4) * P:(k % 4 + 1) * P], ACT.Copy,
                                         scale=gain[:, k:k + 1]).then_inc(evac, 1)
                act.wait_ge(evac, KD * (n + 1))
                act.dma_start(hT_out.rearrange("(k p) t -> p k t", p=P)[:, :, n * P:(n + 1) * P],
                              turned_sb[:, 0]).then_inc(hT_stored, 16)

            for b in range(NBLK):
                for s in range(KD):
                    mix_heads(b * KD + s)
                    if b and s == 1:
                        spill(b * TPB - 1)
                for t in range(TPB):
                    stats(b * TPB + t)
                    if t:
                        spill(b * TPB + t - 1)
            spill(NTOK - 1)
            for s in range(3):
                act.wait_ge(x2_stored[s], 16 * len(range(s, NTOK, 3)))
            act.wait_ge(hT_stored, 16 * NTOK)

        @block.tensor
        def _(pe):
            def branches(b, s):
                n = b * KD + s
                pe.wait_ge(w_tail, w_index(b, "mix", s) + 1)
                for branch in range(2):
                    at_least(pe, multiplied, 2 * (n - 2) + branch + 1)
                    ks = range(branch * KA // 2, (branch + 1) * KA // 2)
                    for k in ks:
                        if s == 0:
                            pe.wait_ge(a_tail, b * KA + k + 1)
                        for a, c in SPLIT:
                            last = nc.tensor.matmul(ps[:, 2 * (n % 2) + branch], w[:, a, s % 2, k], act_s[:, c, k],
                                                    start=(k == ks[0] and (a, c) == SPLIT[0]),
                                                    stop=(k == ks[-1] and (a, c) == SPLIT[-1]))
                    last.then_inc(branch_mm, 1)

            def output(b, t):
                n = b * TPB + t
                for half in range(2):
                    at_least(pe, x2_done, 2 * (n - 1) + half + 1)
                    if t == 0:
                        pe.wait_ge(w_tail, w_index(b, "out", (half + 1) * SPH - 1) + 1)
                    for k in range(KD):
                        if t == 0 and half == 0:
                            pe.wait_ge(mix_tail, b * KD + k + 1)
                        for a, c in SPLIT:
                            last = nc.tensor.matmul(ps[:, 4 + half], mixed[:, a, k, t * P:(t + 1) * P],
                                                    wo[:, c, k, half * SPH:(half + 1) * SPH],
                                                    start=(k == 0 and (a, c) == SPLIT[0]),
                                                    stop=(k == KD - 1 and (a, c) == SPLIT[-1]))
                    last.then_inc(out_mm, 1)

            def turn(n):
                pe.wait_ge(h2_done, n + 1)
                at_least(pe, evac, KD * n)
                for k in range(KD):
                    last = nc.tensor.transpose(ps[:, 6 + k // 4, (k % 4) * P:(k % 4 + 1) * P],
                                               h2[:, n % 2, k * P:(k + 1) * P], ident[:, :])
                last.then_inc(turned, 1)

            pe.wait_ge(const_in, 32)
            for b in range(NBLK):
                for s in range(KD):
                    branches(b, s)
                    if b and s == 1:
                        turn(b * TPB - 1)
                for t in range(TPB):
                    output(b, t)
                    if t:
                        turn(b * TPB + t - 1)
            turn(NTOK - 1)


def conv_ffn_phase(nc, x2, hT, w_up, w_down, conv, final_g, out):
    FK = D_FF // P
    UP = 2 * FK
    DOWN = FK
    PER = UP + DOWN
    ITER = 4
    HALF = D // 2
    W = BLK + 1
    LEAD = P - 1
    TAPS, EDGE, BODY = 0, 4, 6
    CHUNKS = [list(range(max(0, TPB * b - 1), TPB * b + TPB - 1 + (b == NBLK - 1))) for b in range(NBLK)]
    SLOTS = max(len(c) for c in CHUNKS)
    ACC = (4, 5, 6, 7, 0)
    BEFORE = [sum(len(c) for c in CHUNKS[:b]) for b in range(NBLK + 1)]

    def column(b, i):
        return i * P + (P if b == 0 else 0)

    with ExitStack() as ctx:
        m = Pool(nc, ctx, "ff")
        hid = m.sb("hid", [P, 2, FK, BLK + P], F32R)
        h = m.sb("h", [P, 2, KD, BLK], F32R)
        w = m.sb("w", [P, 2, 2, KD * P], F32R)
        wraw = m.sb("wraw", [P, 2, KD * P])
        hraw = m.sb("hraw", [P, 2, BLK])
        y = m.sb("y", [P, SLOTS, D])
        u = m.sb("u", [P, 2, BODY + BLK + 1])
        val = m.sb("val", [P, W])
        gate = m.sb("gate", [P, W])
        gain = m.sb("gain", [P, D])
        param = m.sb("param", [P, UP, BODY])
        square = m.sb("square", [P, D], BF16)
        sumsq, mean, root, rstd, corr, scale = (
            m.sb(s, [P, NTOK]) for s in ("sumsq", "mean", "root", "rstd", "corr", "scale"))
        ps = m.banks()

        const_in, h_in, w_in, y_in = m.sem("const_in"), m.sems("h_in", 2), m.sems("w_in", 2), m.sem("y_in")
        cleared, h_head, h_tail, w_head, w_tail = (
            m.sem(s) for s in ("cleared", "h_head", "h_tail", "w_head", "w_tail"))
        used = m.sem("used")
        copied, edges, conv_done, silu_done, prod_done, hid_head, hid_tail, step = (
            m.sem(s) for s in ("copied", "edges", "conv_done", "silu_done", "prod_done", "hid_head", "hid_tail", "step"))
        step_up = m.sem("step_up")
        shifted_head, shifted_tail = m.sem("shifted_head"), m.sem("shifted_tail")
        added, sumsq_done, mean_done, root_done, y_done, stored = (
            m.sem(s) for s in ("added", "sumsq_done", "mean_done", "root_done", "y_done", "stored"))

        def ge(engine, sem, base, i=0, per=0):
            if isinstance(i, int):
                at_least(engine, sem, base + per * i)
            else:
                engine.wait_ge(sem, i * per + base)

        def up_steps(engine, step_fn, b, extra=None):
            for j in range(2 * ITER):
                step_fn(b, j // ITER, j % ITER)
                if extra:
                    extra(b, j)
            with engine.Fori(2, UP // ITER - 1) as i:
                for j in range(ITER):
                    step_fn(b, i, j)
            for j in range(ITER):
                step_fn(b, UP // ITER - 1, j)

        block = ctx.enter_context(nc.Block())

        @block.sync
        def _(sp):
            sp.dma_start(param[:, :, TAPS:EDGE], conv).then_inc(const_in, 16)
            sp.dma_start(gain[:, :], bass.AP(final_g.tensor, final_g.offset, [[0, P], [1, D]])).then_inc(const_in, 16)

            def load_up(b, i, j):
                ge(sp, w_tail, PER * b + j - 1, i, ITER)
                if isinstance(i, int):
                    src = w_up[ITER * i + j]
                else:
                    src = w_up[bass.ds(i * ITER + j, 1)].rearrange("o p c -> (o p) c")
                sp.dma_start(wraw[:, j % 2], src).then_inc(w_in[j % 2], 16)

            def load_down(b, d):
                sp.wait_ge(w_tail, PER * b + UP + d - 1)
                sp.dma_start(wraw[:, d % 2], w_down[d]).then_inc(w_in[d % 2], 16)

            def load_h(b, k):
                n = b * KD + k
                at_least(sp, h_tail, n - 1)
                sp.dma_start(hraw[:, n % 2], hT[k * P:(k + 1) * P, b * BLK:(b + 1) * BLK]).then_inc(h_in[n % 2], 16)

            def load_y(b, i):
                t = CHUNKS[b][i]
                if b:
                    sp.wait_ge(stored, 16 * BEFORE[b])
                sp.dma_start(y[:, i], x2[t * P:(t + 1) * P, :]).then_inc(y_in, 16)

            def store(b, i):
                n = BEFORE[b] + i
                sp.wait_ge(y_done, n + 1)
                sp.dma_start(out[CHUNKS[b][i] * P:(CHUNKS[b][i] + 1) * P, :], y[:, i]).then_inc(stored, 16)

            for k in range(KD):
                if k in (0, 4):
                    load_up(0, 0, k // 4)
                load_h(0, k)
            for b in range(NBLK):
                load_up(b, 0, 2)
                load_up(b, 0, 3)
                with sp.Fori(1, UP // ITER) as i:
                    for j in range(ITER):
                        load_up(b, i, j)
                load_down(b, 0)
                if b:
                    for i in range(len(CHUNKS[b - 1])):
                        store(b - 1, i)
                for d in range(1, DOWN):
                    load_down(b, d)
                    if d == 2:
                        for i in range(len(CHUNKS[b])):
                            load_y(b, i)
                    if b < NBLK - 1 and 2 < d <= 2 + KD:
                        load_h(b + 1, d - 3)
                if b < NBLK - 1:
                    load_up(b + 1, 0, 0)
                    load_up(b + 1, 0, 1)
            for i in range(len(CHUNKS[-1])):
                store(NBLK - 1, i)
            sp.wait_ge(stored, 16 * NTOK)

        @block.gpsimd
        def _(pool):
            def w_tails(n, slot, i=0, per=0):
                ge(pool, w_head, n + 1, i, per)
                nc.gpsimd.tensor_tensor(w[:, 1, slot], wraw[:, slot], f32(w[:, 0, slot]), ALU.subtract).then_inc(w_tail, 1)

            def h_tails(b, k):
                n = b * KD + k
                pool.wait_ge(h_head, n + 1)
                nc.gpsimd.tensor_tensor(h[:, 1, k], hraw[:, n % 2], f32(h[:, 0, k]), ALU.subtract).then_inc(h_tail, 1)

            for k in range(KD):
                if k in (0, 4):
                    w_tails(k // 4, k // 4)
                h_tails(0, k)
            for b in range(NBLK):
                w_tails(PER * b + 2, 0)
                w_tails(PER * b + 3, 1)
                with pool.Fori(1, UP // ITER) as i:
                    for j in range(ITER):
                        w_tails(PER * b + j, j % 2, i, ITER)
                for d in range(DOWN + 2 * (b < NBLK - 1)):
                    w_tails(PER * b + UP + d, d % 2)
                    if b < NBLK - 1 and 3 <= d < 3 + KD:
                        h_tails(b + 1, d - 3)

        @block.vector
        def _(dve):
            V = nc.vector
            steps = [0]

            def after(ins):
                steps[0] += 1
                ins.then_inc(step, 1)
                dve.wait_ge(step, steps[0])

            def w_heads(b, t, i=0, per=0):
                n = PER * b + t
                ge(dve, w_in[t % 2], 16 * (n // 2 + 1), i, 16 * per // 2)
                ge(dve, used, n - 1, i, per)
                V.tensor_copy(w[:, 0, t % 2], wraw[:, t % 2]).then_inc(w_head, 1)

            def h_heads(b, k):
                n = b * KD + k
                dve.wait_ge(h_in[n % 2], 16 * (n // 2 + 1))
                at_least(dve, used, PER * (b - 1) + UP if b else 0)
                V.tensor_copy(h[:, 0, k], hraw[:, n % 2]).then_inc(h_head, 1)

            def up_step(b, i, j):
                w_heads(b, j + 2, i, ITER)
                t = UP * b + j
                par = lambda: param[:, ITER * i + j] if isinstance(i, int) else (
                    param[:, bass.ds(i * ITER + j, 1)].rearrange("p o c -> p (o c)"))
                s = j % 2
                dst = (val, gate)[s]
                k = 2 * i + j // 2 if isinstance(i, int) else None
                hk = lambda part: hid[:, part, k, LEAD:] if k is not None else (
                    hid[:, part, bass.ds(i * 2 + j // 2, 1), LEAD:].rearrange("p o c -> p (o c)"))
                ge(dve, conv_done, t - 1, i, ITER)
                V.tensor_scalar(u[:, s, TAPS:BODY], par(), 1.0, None, ALU.mult).then_inc(edges, 1)
                ge(dve, copied, t + 1, i, ITER)
                ge(dve, edges, 2 * t + 1, i, 2 * ITER)
                V.tensor_scalar(par()[:, EDGE:], u[:, s, BODY + BLK - 2:BODY + BLK], 1.0, None, ALU.mult).then_inc(edges, 1)
                tap = lambda q: u[:, s, TAPS + q:TAPS + q + 1]
                ge(dve, prod_done, (t - 1) // 2 if s == 0 else (t + 1) // 2 - 1, i, ITER // 2)
                if s:
                    ge(dve, prod_done, (t - 1) // 2, i, ITER // 2)
                V.tensor_scalar(dst[:, :], u[:, s, EDGE + 1:EDGE + 1 + W], tap(1), tap(3), ALU.mult, ALU.add
                                ).then_inc(step_up, 1)
                ge(dve, step_up, 2 * t + 1, i, 2 * ITER)
                V.scalar_tensor_tensor(out=dst[:, :], in0=u[:, s, EDGE:EDGE + W], scalar=tap(0), in1=dst[:, :],
                                       op0=ALU.mult, op1=ALU.add).then_inc(step_up, 1)
                ge(dve, step_up, 2 * t + 2, i, 2 * ITER)
                ge(dve, edges, 2 * t + 2, i, 2 * ITER)
                V.scalar_tensor_tensor(out=dst[:, :], in0=u[:, s, EDGE + 2:EDGE + 2 + W], scalar=tap(2), in1=dst[:, :],
                                       op0=ALU.mult, op1=ALU.add).then_inc(conv_done, 1)
                if s:
                    p = (t - 1) // 2
                    ge(dve, silu_done, p + 1, i, ITER // 2)
                    V.tensor_tensor(val[:, :], val[:, :], gate[:, :], ALU.mult).then_inc(prod_done, 1)
                    ge(dve, prod_done, p + 1, i, ITER // 2)
                    V.tensor_scalar(hk(0), val[:, :], 1.0, None, ALU.mult).then_inc(hid_head, 1)
                    ge(dve, hid_head, p + 1, i, ITER // 2)
                    V.tensor_tensor(hk(1), val[:, :], f32(hk(0)), ALU.subtract).then_inc(hid_tail, 1)
                    ge(dve, hid_tail, p + 1, i, ITER // 2)

            def add(b, half):
                for i in range(len(CHUNKS[b])):
                    if half == 0:
                        dve.wait_ge(y_in, 16 * BEFORE[b + 1])
                    add_one(b, half, i)

            def add_one(b, half, i):
                dve.wait_ge(used, PER * b + UP + (half + 1) * (DOWN // 2))
                part = y[:, i, half * HALF:(half + 1) * HALF]
                V.tensor_tensor(part, ps[:, ACC[i]], part, ALU.add).then_inc(added, 1)

            def finish(b, i):
                n = BEFORE[b] + i
                c = slice(n, n + 1)
                dve.wait_ge(sumsq_done, n + 1)
                V.tensor_scalar(mean[:, c], sumsq[:, c], 1.0 / D, EPS, ALU.mult, ALU.add).then_inc(mean_done, 1)
                dve.wait_ge(root_done, n + 1)
                after(V.reciprocal(rstd[:, c], root[:, c]))
                after(V.tensor_scalar(corr[:, c], rstd[:, c], rstd[:, c], mean[:, c], ALU.mult, ALU.mult))
                after(V.tensor_scalar(scale[:, c], corr[:, c], -0.5, 1.5, ALU.mult, ALU.add))
                after(V.tensor_tensor(rstd[:, c], rstd[:, c], scale[:, c], ALU.mult))
                V.scalar_tensor_tensor(out=y[:, i], in0=y[:, i], scalar=rstd[:, c], in1=gain[:, :],
                                       op0=ALU.mult, op1=ALU.mult).then_inc(y_done, 1)

            def extra(b, j):
                i = j // 2
                if b and i < len(CHUNKS[b - 1]):
                    if j % 2 == 0:
                        add_one(b - 1, 1, i)
                    else:
                        finish(b - 1, i)

            V.memset(param[:, :, EDGE:BODY], 0.0).then_inc(cleared, 1)
            V.memset(hid[:, :, :, 0:LEAD].bitcast(F32), 0.0).then_inc(cleared, 1)
            V.memset(u[:, :, BODY + BLK:], 0.0).then_inc(cleared, 1)
            dve.wait_ge(cleared, 3)
            dve.wait_ge(const_in, 32)
            for k in range(KD):
                if k in (0, 4):
                    w_heads(0, k // 4)
                h_heads(0, k)
            for b in range(NBLK):
                up_steps(dve, up_step, b, extra)
                for d in range(DOWN):
                    if d < DOWN - 2:
                        w_heads(b, UP + d + 2)
                    elif b < NBLK - 1:
                        w_heads(b + 1, d - (DOWN - 2))
                    if d == DOWN // 2 - 1:
                        add(b, 0)
                    if b < NBLK - 1 and 1 <= d < 1 + KD:
                        h_heads(b + 1, d - 1)
                if b < NBLK - 1:
                    dve.wait_ge(used, PER * (b + 1))
                    V.tensor_copy(hid[:, 0, :, 0:LEAD], f32(hid[:, 0, :, BLK:BLK + LEAD])).then_inc(shifted_head, 1)
                    dve.wait_ge(shifted_head, b + 1)
                    dve.wait_ge(shifted_tail, b + 1)
            add_one(NBLK - 1, 1, 0)
            for i in range(len(CHUNKS[-1])):
                if i + 1 < len(CHUNKS[-1]):
                    add_one(NBLK - 1, 1, i + 1)
                finish(NBLK - 1, i)

        @block.scalar
        def _(act):
            def up_step(b, i, j):
                t = UP * b + j
                s = j % 2
                ge(act, used, PER * b + j + 1, i, ITER)
                ge(act, conv_done, t - 1, i, ITER)
                nc.scalar.activation(u[:, s, BODY:BODY + BLK], ps[:, j], ACT.Copy).then_inc(copied, 1)
                if s:
                    ge(act, conv_done, t + 1, i, ITER)
                    nc.scalar.activation(gate[:, :], gate[:, :], ACT.Silu).then_inc(silu_done, 1)

            def squares(b, i):
                n = BEFORE[b] + i
                act.wait_ge(added, BEFORE[b + 1] + n + 1)
                at_least(act, sumsq_done, n)
                nc.scalar.activation(square[:, :], y[:, i], ACT.Square, accum_out=sumsq[:, n:n + 1]).then_inc(sumsq_done, 1)

            def square_root(b, i):
                n = BEFORE[b] + i
                act.wait_ge(mean_done, n + 1)
                nc.scalar.activation(root[:, n:n + 1], mean[:, n:n + 1], ACT.Sqrt).then_inc(root_done, 1)

            def extra(b, j):
                if b and j // 2 < len(CHUNKS[b - 1]):
                    (squares, square_root)[j % 2](b - 1, j // 2)

            for b in range(NBLK):
                up_steps(act, up_step, b, extra)
                if b < NBLK - 1:
                    act.wait_ge(used, PER * (b + 1))
                    act.wait_ge(hid_tail, FK * (b + 1))
                    nc.scalar.activation(hid[:, 1, :, 0:LEAD], f32(hid[:, 1, :, BLK:BLK + LEAD]), ACT.Copy).then_inc(shifted_tail, 1)
            for i in range(len(CHUNKS[-1])):
                squares(NBLK - 1, i)
                square_root(NBLK - 1, i)

        @block.tensor
        def _(pe):
            def up_step(b, i, j):
                t = UP * b + j
                ge(pe, w_tail, PER * b + j + 1, i, ITER)
                ge(pe, copied, t - 3, i, ITER)
                for k in range(KD):
                    if isinstance(i, int) and i == 0 and j == 0:
                        pe.wait_ge(h_tail, b * KD + k + 1)
                    for a, c in SPLIT:
                        last = nc.tensor.matmul(ps[:, j], w[:, a, j % 2, k * P:(k + 1) * P], h[:, c, k],
                                                start=(k == 0 and (a, c) == SPLIT[0]),
                                                stop=(k == KD - 1 and (a, c) == SPLIT[-1]))
                last.then_inc(used, 1)

            def down(b):
                for d in range(DOWN):
                    half, pair = divmod(d, DOWN // 2)
                    pe.wait_ge(w_tail, PER * b + UP + d + 1)
                    for q in range(2):
                        k = 2 * pair + q
                        if half == 0:
                            pe.wait_ge(hid_tail, FK * b + k + 1)
                            if b and d == 0 and q == 0:
                                pe.wait_ge(shifted_head, b)
                                pe.wait_ge(shifted_tail, b)
                        for i in range(len(CHUNKS[b])):
                            if pair == 0 and q == 0:
                                if half:
                                    pe.wait_ge(added, 2 * BEFORE[b] + i + 1)
                                elif b:
                                    pe.wait_ge(added, 2 * BEFORE[b])
                                if i == TPB:
                                    pe.wait_ge(copied, UP * (b + 1))
                            c0 = column(b, i)
                            for a, c in SPLIT:
                                last = nc.tensor.matmul(ps[:, ACC[i]], hid[:, a, k, c0:c0 + P],
                                                        w[:, c, d % 2, q * HALF:(q + 1) * HALF],
                                                        start=(k == 0 and (a, c) == SPLIT[0]),
                                                        stop=(k == FK - 1 and (a, c) == SPLIT[-1]))
                    last.then_inc(used, 1)

            for b in range(NBLK):
                up_steps(pe, up_step, b)
                down(b)


def encoder_layer(nc, x, w_in, norm1_g, b_gate, rpb, w_mix, w_out, norm2_g, w_up, w_down, conv, final_g,
                  pos_table, chan_table, mask, eye, out):
    def scratch(name, *shape):
        return nc.dram_tensor(name, shape, F32, kind="Internal").ap()

    u, v = scratch("u", SEQ, FNET_W), scratch("v", SEQ, NA_W)
    qT, kT = scratch("qT", NA_W, SEQ), scratch("kT", NA_W, SEQ)
    gT = scratch("gT", 2 * D, SEQ)
    fnT, atT = scratch("fnT", FNET_W, SEQ), scratch("atT", NA_W, SEQ)
    x2, hT = scratch("x2", SEQ, D), scratch("hT", D, SEQ)
    padded = scratch("padded", HEADS, REL_R, REL_C)
    shifted = scratch("shifted", KINDS, HEADS, QC, REL_R, KC)

    input_phase(nc, x, w_in, norm1_g, b_gate, eye, u, qT, v, kT, gT)
    fourier_phase(nc, u, pos_table, chan_table, fnT, rpb, padded, shifted)
    attention_phase(nc, qT, kT, v, shifted, mask, eye, atT)
    mixer_output_phase(nc, x, fnT, atT, gT, w_mix, w_out, norm2_g, eye, x2, hT)
    conv_ffn_phase(nc, x2, hT, w_up, w_down, conv, final_g, out)


def column_tiles(w):
    return w.reshape(KD, P, -1, P).transpose(2, 1, 0, 3)


def kernel(x, norm1_g, w_in, b_gate, rpb, w_fa, w_nb, w_out, norm2_g, w_up, conv_w, conv_b, w_down, final_g):
    import concourse.bacc as _bacc
    from concourse.bass_utils import run_bass_kernel_spmd as _run

    x, norm1_g, w_in, b_gate, rpb, w_fa, w_nb, w_out, norm2_g, w_up, conv_w, conv_b, w_down, final_g = (
        np.asarray(a) for a in (x, norm1_g, w_in, b_gate, rpb, w_fa, w_nb, w_out, norm2_g, w_up, conv_w, conv_b,
                                w_down, final_g))
    pos, chan = fourier_tables()
    taps = np.concatenate([conv_w[0], conv_b], axis=0)
    layout = {
        "x": x.reshape(SEQ, D),
        "w_in": column_tiles(w_in[0]),
        "norm1_g": norm1_g[0],
        "b_gate": b_gate[0].reshape(2 * KD, P).T,
        "rpb": rpb[0],
        "w_mix": column_tiles(np.concatenate([w_fa[0], w_nb[0]], axis=0)),
        "w_out": column_tiles(w_out[0]),
        "norm2_g": norm2_g[0].reshape(KD, P).T,
        "w_up": w_up[0].reshape(KD, P, 2, D_FF // P, P).transpose(3, 2, 1, 0, 4).reshape(2 * D_FF // P, P, D),
        "w_down": w_down[0].reshape(D_FF // (2 * P), 2, P, 2, D // 2).transpose(3, 0, 2, 1, 4).reshape(D_FF // P, P, D),
        "conv": taps.reshape(4, 2, D_FF // P, P).transpose(3, 2, 1, 0).reshape(P, 2 * D_FF // P, 4),
        "final_g": final_g,
        "pos_table": pos,
        "chan_table": chan,
        "mask": window_mask(),
        "eye": np.eye(P, dtype=np.float32),
    }
    nc = _bacc.Bacc("TRN2", target_bir_lowering=False, num_devices=1)
    arrays, args = {}, []
    for name, a in layout.items():
        arrays[f"in_{name}_dram"] = np.ascontiguousarray(a)
        args.append(nc.dram_tensor(f"in_{name}_dram", a.shape, F32, kind="ExternalInput").ap())
    args.append(nc.dram_tensor("out_0_dram", (SEQ, D), F32, kind="ExternalOutput").ap())
    encoder_layer(nc, *args)
    r = _run(nc, [arrays], core_ids=[0])
    return np.asarray(r.results[0]["out_0_dram"]).reshape(x.shape)
```
